# Optimizing a Trainium2 kernel written in Bass

```python
import math
import jax, jax.numpy as jnp
from jax import lax
import numpy as np

D_MODEL = 1024
BATCH = 1
SEQ = 256
DEPTH = 1

HEAD_DIM = 64
N_HEADS_TOTAL = D_MODEL // HEAD_DIM
N_HEADS_MOBA = N_HEADS_TOTAL // 2
N_HEADS_SWA = N_HEADS_TOTAL - N_HEADS_MOBA
N_KV_SWA = 2
GQA_GROUP = N_HEADS_SWA // N_KV_SWA
MIX_WIDTH = N_HEADS_TOTAL * HEAD_DIM
MOBA_BLOCK = 256
MOBA_TOPK = 3
MOBA_QCHUNK = 16
SWA_WINDOW = 128
N_BUCKETS = 32
MAX_DISTANCE = 128
D_FF = 4 * D_MODEL
EPS = 1e-6
W_A = N_HEADS_MOBA * HEAD_DIM
W_QB = N_HEADS_SWA * HEAD_DIM
W_KVB = N_KV_SWA * HEAD_DIM
D_IN = 3 * W_A + W_QB + 2 * W_KVB


def rmsnorm(x, g):
    xf = x.astype(jnp.float32)
    y = xf * lax.rsqrt(jnp.mean(xf * xf, axis=-1, keepdims=True) + EPS)
    return (y * g.astype(jnp.float32)).astype(x.dtype)

def t5_bucket(dist):
    n = jnp.maximum(dist, 0)
    max_exact = N_BUCKETS // 2
    nf = jnp.maximum(n, 1).astype(jnp.float32)
    large = max_exact + (jnp.log(nf / max_exact) / math.log(MAX_DISTANCE / max_exact)
                         * (N_BUCKETS - max_exact)).astype(jnp.int32)
    large = jnp.minimum(large, N_BUCKETS - 1)
    return jnp.where(n < max_exact, n, large)

def moba_attention(q, k, v, bias_hb):
    B, H, S, dh = q.shape
    nb = -(-S // MOBA_BLOCK)
    sp = nb * MOBA_BLOCK
    padw = ((0, 0), (0, 0), (0, sp - S), (0, 0))
    q, k, v = jnp.pad(q, padw), jnp.pad(k, padw), jnp.pad(v, padw)
    kb = k.reshape(B, H, nb, MOBA_BLOCK, dh)
    vb = v.reshape(B, H, nb, MOBA_BLOCK, dh)
    k_mean = jnp.mean(kb.astype(jnp.float32), axis=3)
    gate = jnp.einsum('bhsd,bhnd->bhsn', q.astype(jnp.float32), k_mean)
    q_block = jnp.arange(sp) // MOBA_BLOCK
    fully_past = jnp.arange(nb)[None, :] < q_block[:, None]
    gate = jnp.where(fully_past, gate, -jnp.inf)
    n_sel = min(MOBA_TOPK, nb)
    sel_score, sel_idx = lax.top_k(gate, n_sel)
    sel_valid = jnp.isfinite(sel_score)
    scale = dh ** -0.5
    b_idx = jnp.arange(B)[:, None, None, None]
    h_idx = jnp.arange(H)[None, :, None, None]
    offs = jnp.arange(MOBA_BLOCK)

    def chunk(ci):
        q0 = ci * MOBA_QCHUNK
        qc = lax.dynamic_slice_in_dim(q, q0, MOBA_QCHUNK, axis=2)
        idx = lax.dynamic_slice_in_dim(sel_idx, q0, MOBA_QCHUNK, axis=2)
        valid = lax.dynamic_slice_in_dim(sel_valid, q0, MOBA_QCHUNK, axis=2)
        qpos = q0 + jnp.arange(MOBA_QCHUNK)
        k_sel = kb[b_idx, h_idx, idx]
        v_sel = vb[b_idx, h_idx, idx]
        s_sel = jnp.einsum('bhqd,bhqnjd->bhqnj', qc, k_sel).astype(jnp.float32) * scale
        kpos_sel = idx[..., None] * MOBA_BLOCK + offs
        s_sel = s_sel + bias_hb[h_idx[..., None], t5_bucket(qpos[:, None, None] - kpos_sel)]
        s_sel = jnp.where(valid[..., None], s_sel, -jnp.inf)
        ob = q0 // MOBA_BLOCK
        k_own = lax.dynamic_slice_in_dim(k, ob * MOBA_BLOCK, MOBA_BLOCK, axis=2)
        v_own = lax.dynamic_slice_in_dim(v, ob * MOBA_BLOCK, MOBA_BLOCK, axis=2)
        s_own = jnp.einsum('bhqd,bhjd->bhqj', qc, k_own).astype(jnp.float32) * scale
        dist = qpos[:, None] - (ob * MOBA_BLOCK + offs)[None, :]
        s_own = s_own + bias_hb[:, t5_bucket(dist)][None]
        s_own = jnp.where(dist >= 0, s_own, -jnp.inf)
        logits = jnp.concatenate(
            [s_sel.reshape(B, H, MOBA_QCHUNK, n_sel * MOBA_BLOCK), s_own], axis=-1)
        p = jax.nn.softmax(logits, axis=-1)
        p_sel = p[..., :n_sel * MOBA_BLOCK].reshape(B, H, MOBA_QCHUNK, n_sel, MOBA_BLOCK).astype(v.dtype)
        p_own = p[..., n_sel * MOBA_BLOCK:].astype(v.dtype)
        return (jnp.einsum('bhqnj,bhqnjd->bhqd', p_sel, v_sel)
                + jnp.einsum('bhqj,bhjd->bhqd', p_own, v_own))

    outs = lax.map(chunk, jnp.arange(sp // MOBA_QCHUNK))
    out = jnp.moveaxis(outs, 0, 2).reshape(B, H, sp, dh)
    return out[:, :, :S]

def swa_attention(q, k, v, bias_hb, sinks):
    B, HKV, G, S, dh = q.shape
    W = SWA_WINDOW
    nbq = S // W
    qb = q.reshape(B, HKV, G, nbq, W, dh)
    kb = k.reshape(B, HKV, nbq, W, dh)
    vb = v.reshape(B, HKV, nbq, W, dh)
    pad_prev = ((0, 0), (0, 0), (1, 0), (0, 0), (0, 0))
    k_band = jnp.concatenate([jnp.pad(kb[:, :, :-1], pad_prev), kb], axis=3)
    v_band = jnp.concatenate([jnp.pad(vb[:, :, :-1], pad_prev), vb], axis=3)
    s = jnp.einsum('bkgnqd,bknjd->bkgnqj', qb, k_band).astype(jnp.float32) * (dh ** -0.5)
    blk = jnp.arange(nbq)
    qpos = blk[:, None] * W + jnp.arange(W)[None, :]
    kpos = (blk[:, None] - 1) * W + jnp.arange(2 * W)[None, :]
    dist = qpos[:, :, None] - kpos[:, None, :]
    allowed = (dist >= 0) & (dist < W) & (kpos[:, None, :] >= 0)
    bias = bias_hb[:, t5_bucket(dist)].reshape(HKV, G, nbq, W, 2 * W)
    s = jnp.where(allowed, s + bias, -jnp.inf)
    sink = jnp.broadcast_to(sinks.astype(jnp.float32).reshape(1, HKV, G, 1, 1, 1), s.shape[:-1] + (1,))
    p = jax.nn.softmax(jnp.concatenate([s, sink], axis=-1), axis=-1)[..., :-1]
    out = jnp.einsum('bkgnqj,bknjd->bkgnqd', p.astype(v.dtype), v_band)
    return out.reshape(B, HKV, G, S, dh)

def token_mixer(h, w_in, w_out, sinks, bias_hb):
    B, S, _ = h.shape
    proj = h @ w_in
    qa, ka, va, qb, kb, vb = jnp.split(
        proj, [W_A, 2 * W_A, 3 * W_A, 3 * W_A + W_QB, 3 * W_A + W_QB + W_KVB], axis=-1)
    heads = lambda t, n: t.reshape(B, S, n, HEAD_DIM).transpose(0, 2, 1, 3)
    out_a = moba_attention(heads(qa, N_HEADS_MOBA), heads(ka, N_HEADS_MOBA),
                           heads(va, N_HEADS_MOBA), bias_hb[:N_HEADS_MOBA])
    out_a = out_a.transpose(0, 2, 1, 3).reshape(B, S, W_A)
    q_swa = qb.reshape(B, S, N_KV_SWA, GQA_GROUP, HEAD_DIM).transpose(0, 2, 3, 1, 4)
    out_b = swa_attention(q_swa, heads(kb, N_KV_SWA), heads(vb, N_KV_SWA),
                          bias_hb[N_HEADS_MOBA:], sinks)
    out_b = out_b.transpose(0, 3, 1, 2, 4).reshape(B, S, W_QB)
    return jnp.concatenate([out_a, out_b], axis=-1) @ w_out

def first_inputs(seed: int = 0) -> dict:
    key = jax.random.key(seed)
    ks = jax.random.split(key, 13)
    f32 = jnp.float32
    nrm = lambda k, shape, s: jax.random.normal(k, shape, f32) * s
    return {
        "x": nrm(ks[0], (BATCH, SEQ, D_MODEL), 1.0),
        "c": nrm(ks[1], (BATCH, D_MODEL), 1.0),
        "w_in": nrm(ks[2], (DEPTH, D_MODEL, D_IN), D_MODEL ** -0.5),
        "w_out": nrm(ks[3], (DEPTH, MIX_WIDTH, D_MODEL), MIX_WIDTH ** -0.5),
        "sinks": nrm(ks[4], (DEPTH, N_HEADS_SWA), 0.5),
        "rel_bias": nrm(ks[5], (N_BUCKETS, N_HEADS_TOTAL), 0.5),
        "w_ada": nrm(ks[6], (DEPTH, D_MODEL, 6 * D_MODEL), D_MODEL ** -0.5),
        "b_ada": nrm(ks[7], (DEPTH, 6 * D_MODEL), 0.02),
        "norm_gains": 1.0 + nrm(ks[8], (DEPTH, 4, D_MODEL), 0.05),
        "w1": nrm(ks[9], (DEPTH, D_MODEL, D_FF), D_MODEL ** -0.5),
        "b1": nrm(ks[10], (DEPTH, D_FF), 0.02),
        "w2": nrm(ks[11], (DEPTH, D_FF, D_MODEL), D_FF ** -0.5),
        "b2": nrm(ks[12], (DEPTH, D_MODEL), 0.02),
    }

def first_block(x, c, w_in, w_out, sinks, rel_bias, w_ada, b_ada, norm_gains, w1, b1, w2, b2):
    bias_hb = rel_bias.T
    c_act = jax.nn.silu(c)
    for l in range(DEPTH):
        mod = c_act @ w_ada[l] + b_ada[l]
        sh1, sc1, g1, sh2, sc2, g2 = [m[:, None, :] for m in jnp.split(mod, 6, axis=-1)]
        h = rmsnorm(x, norm_gains[l, 0]) * (1.0 + sc1) + sh1
        y = token_mixer(h, w_in[l], w_out[l], sinks[l], bias_hb)
        x = x + g1 * rmsnorm(y, norm_gains[l, 1])
        h = rmsnorm(x, norm_gains[l, 2]) * (1.0 + sc2) + sh2
        y = jnp.square(jax.nn.relu(h @ w1[l] + b1[l])) @ w2[l] + b2[l]
        x = x + g2 * rmsnorm(y, norm_gains[l, 3])
    return x


MIX_WIDTH_2 = 256
CONV_K = 3
GMLP_GROUPS = 4
GMLP_CHUNK = 128
SB_HEADS = MIX_WIDTH_2 // HEAD_DIM
FOX_HEADS = MIX_WIDTH_2 // HEAD_DIM
Q_BLOCK = 128
N_BRANCH = 4
FFN_HIDDEN = -(-8 * D_MODEL // (3 * 256)) * 256
IN_SPLIT_SIZES = (MIX_WIDTH_2, MIX_WIDTH_2, MIX_WIDTH_2, 2 * MIX_WIDTH_2, MIX_WIDTH_2, MIX_WIDTH_2, MIX_WIDTH_2,
                  MIX_WIDTH_2, MIX_WIDTH_2, MIX_WIDTH_2, FOX_HEADS, N_BRANCH * D_MODEL)
N_IN = sum(IN_SPLIT_SIZES)


def _rms_norm(x, g):
    xf = x.astype(jnp.float32)
    y = xf * lax.rsqrt(jnp.mean(xf * xf, axis=-1, keepdims=True) + EPS)
    return (y * g.astype(jnp.float32)).astype(x.dtype)

def _layer_norm(x, g, b):
    xf = x.astype(jnp.float32)
    mu = jnp.mean(xf, axis=-1, keepdims=True)
    var = jnp.mean(jnp.square(xf - mu), axis=-1, keepdims=True)
    y = (xf - mu) * lax.rsqrt(var + EPS)
    return (y * g.astype(jnp.float32) + b.astype(jnp.float32)).astype(x.dtype)

def _split_heads(t, n_heads):
    b, s, _ = t.shape
    return t.reshape(b, s, n_heads, HEAD_DIM).transpose(0, 2, 1, 3)

def _merge_heads(t):
    b, h, s, d = t.shape
    return t.transpose(0, 2, 1, 3).reshape(b, s, h * d)

def _short_conv_mixer(b_gate, c_gate, xt, w_conv):
    xc = c_gate * xt
    y = lax.conv_general_dilated(
        xc, w_conv[:, None, :].astype(xc.dtype), window_strides=(1,),
        padding=[(CONV_K - 1, 0)], dimension_numbers=('NWC', 'WIO', 'NWC'),
        feature_group_count=MIX_WIDTH_2)
    return b_gate * y

def _spatial_gating_mixer(uv, w_s, b_s, ln_g, ln_b):
    u, v = jnp.split(jax.nn.gelu(uv), 2, axis=-1)
    v = _layer_norm(v, ln_g, ln_b)
    bsz, s, _ = v.shape
    v = v.reshape(bsz, s // GMLP_CHUNK, GMLP_CHUNK, GMLP_GROUPS, MIX_WIDTH_2 // GMLP_GROUPS)
    w_causal = jnp.tril(w_s).astype(v.dtype)
    mixed = jnp.einsum('gts,bcsge->bctge', w_causal, v) + b_s.T[None, None, :, :, None].astype(v.dtype)
    return u * mixed.reshape(bsz, s, MIX_WIDTH_2)

def _stick_breaking_attention(q, k, v):
    seq = q.shape[2]
    scale = HEAD_DIM ** -0.5
    outs = []
    for i in range(seq // Q_BLOCK):
        start, end = i * Q_BLOCK, (i + 1) * Q_BLOCK
        z = jnp.einsum('bhqd,bhkd->bhqk', q[:, :, start:end], k[:, :, :end]).astype(jnp.float32) * scale
        q_pos = start + jnp.arange(Q_BLOCK)[:, None]
        k_pos = jnp.arange(end)[None, :]
        strict = k_pos < q_pos
        log_1m_beta = jnp.where(strict, jax.nn.log_sigmoid(-z), 0.0)
        later = lax.cumsum(log_1m_beta, axis=3, reverse=True) - log_1m_beta
        w = jnp.where(strict, jnp.exp(jax.nn.log_sigmoid(z) + later), 0.0)
        outs.append(jnp.einsum('bhqk,bhkd->bhqd', w.astype(v.dtype), v[:, :, :end]))
    return jnp.concatenate(outs, axis=2)

def _forgetting_attention(q, k, v, log_f_cum):
    seq = q.shape[2]
    scale = HEAD_DIM ** -0.5
    neg = jnp.finfo(jnp.float32).min
    outs = []
    for i in range(seq // Q_BLOCK):
        start, end = i * Q_BLOCK, (i + 1) * Q_BLOCK
        logits = jnp.einsum('bhqd,bhkd->bhqk', q[:, :, start:end], k[:, :, :end]).astype(jnp.float32) * scale
        logits = logits + log_f_cum[:, :, start:end, None] - log_f_cum[:, :, None, :end]
        causal = jnp.arange(end)[None, :] <= (start + jnp.arange(Q_BLOCK)[:, None])
        p = jax.nn.softmax(jnp.where(causal, logits, neg), axis=-1)
        outs.append(jnp.einsum('bhqk,bhkd->bhqd', p.astype(v.dtype), v[:, :, :end]))
    return jnp.concatenate(outs, axis=2)

def _mixer_block(xn, w_in, w_conv, w_s, b_s, ln_g, ln_b, q_norm_g, k_norm_g, b_f, w_branch, w_out):
    bsz, s, _ = xn.shape
    proj = xn @ w_in
    idx, acc = [], 0
    for size in IN_SPLIT_SIZES[:-1]:
        acc += size
        idx.append(acc)
    (cb, cc, cx, uv, sb_q, sb_k, sb_v, fx_q, fx_k, fx_v, f_raw, gate_raw) = jnp.split(proj, idx, axis=-1)

    y_a = _short_conv_mixer(cb, cc, cx, w_conv)
    y_b = _spatial_gating_mixer(uv, w_s, b_s, ln_g, ln_b)
    y_c = _merge_heads(_stick_breaking_attention(
        _split_heads(sb_q, SB_HEADS), _split_heads(sb_k, SB_HEADS), _split_heads(sb_v, SB_HEADS)))
    fq = _rms_norm(_split_heads(fx_q, FOX_HEADS), q_norm_g)
    fk = _rms_norm(_split_heads(fx_k, FOX_HEADS), k_norm_g)
    log_f = jax.nn.log_sigmoid((f_raw + b_f).astype(jnp.float32)).transpose(0, 2, 1)
    y_d = _merge_heads(_forgetting_attention(fq, fk, _split_heads(fx_v, FOX_HEADS), lax.cumsum(log_f, axis=2)))

    ys = jnp.stack([y_a, y_b, y_c, y_d], axis=2)
    branches = jnp.einsum('bsnc,ncd->bsnd', ys, w_branch)
    gates = jax.nn.sigmoid(gate_raw.reshape(bsz, s, N_BRANCH, D_MODEL).astype(jnp.float32)).astype(xn.dtype)
    merged = jnp.sum(gates * branches, axis=2)
    return merged @ w_out

def _swiglu(x, w_in, w_out):
    g, u = jnp.split(x @ w_in, 2, axis=-1)
    return (jax.nn.silu(g) * u) @ w_out

def second_inputs(seed: int = 0) -> dict:
    key = jax.random.key(seed)
    ks = jax.random.split(key, 16)
    f32 = jnp.float32
    nrm = lambda k, shape: jax.random.normal(k, shape, f32)
    return {
        'x': nrm(ks[0], (BATCH, SEQ, D_MODEL)),
        'norm_mix_g': 1.0 + 0.05 * nrm(ks[1], (DEPTH, D_MODEL)),
        'w_in': nrm(ks[2], (DEPTH, D_MODEL, N_IN)) * D_MODEL ** -0.5,
        'w_conv': nrm(ks[3], (DEPTH, CONV_K, MIX_WIDTH_2)) * CONV_K ** -0.5,
        'w_spatial': nrm(ks[4], (DEPTH, GMLP_GROUPS, GMLP_CHUNK, GMLP_CHUNK)) * GMLP_CHUNK ** -0.5,
        'b_spatial': 1.0 + 0.1 * nrm(ks[5], (DEPTH, GMLP_GROUPS, GMLP_CHUNK)),
        'gmlp_ln_g': 1.0 + 0.05 * nrm(ks[6], (DEPTH, MIX_WIDTH_2)),
        'gmlp_ln_b': 0.02 * nrm(ks[7], (DEPTH, MIX_WIDTH_2)),
        'fox_q_norm_g': 1.0 + 0.05 * nrm(ks[8], (DEPTH, HEAD_DIM)),
        'fox_k_norm_g': 1.0 + 0.05 * nrm(ks[9], (DEPTH, HEAD_DIM)),
        'fox_forget_b': 2.0 + 0.5 * nrm(ks[10], (DEPTH, FOX_HEADS)),
        'w_branch': nrm(ks[11], (DEPTH, N_BRANCH, MIX_WIDTH_2, D_MODEL)) * MIX_WIDTH_2 ** -0.5,
        'w_out': nrm(ks[12], (DEPTH, D_MODEL, D_MODEL)) * D_MODEL ** -0.5,
        'norm_ffn_g': 1.0 + 0.05 * nrm(ks[13], (DEPTH, D_MODEL)),
        'w_ffn_in': nrm(ks[14], (DEPTH, D_MODEL, 2 * FFN_HIDDEN)) * D_MODEL ** -0.5,
        'w_ffn_out': nrm(ks[15], (DEPTH, FFN_HIDDEN, D_MODEL)) * FFN_HIDDEN ** -0.5,
    }

def second_block(x, norm_mix_g, w_in, w_conv, w_spatial, b_spatial, gmlp_ln_g, gmlp_ln_b,
              fox_q_norm_g, fox_k_norm_g, fox_forget_b, w_branch, w_out, norm_ffn_g,
              w_ffn_in, w_ffn_out):
    h = x
    for l in range(DEPTH):
        xn = _rms_norm(h, norm_mix_g[l])
        h = h + _mixer_block(xn, w_in[l], w_conv[l], w_spatial[l], b_spatial[l], gmlp_ln_g[l],
                             gmlp_ln_b[l], fox_q_norm_g[l], fox_k_norm_g[l], fox_forget_b[l],
                             w_branch[l], w_out[l])
        h = h + _swiglu(_rms_norm(h, norm_ffn_g[l]), w_ffn_in[l], w_ffn_out[l])
    return h


def setup_inputs(seed=0):
    out = dict(first_inputs(seed))
    for name, value in second_inputs(seed + 1).items():
        if name != "x":
            out[name + "_2"] = value
    return out


def reference(
    x, c, w_in, w_out, sinks, rel_bias, w_ada, b_ada, norm_gains, w1, b1, w2, b2, norm_mix_g_2,
    w_in_2, w_conv_2, w_spatial_2, b_spatial_2, gmlp_ln_g_2, gmlp_ln_b_2, fox_q_norm_g_2,
    fox_k_norm_g_2, fox_forget_b_2, w_branch_2, w_out_2, norm_ffn_g_2, w_ffn_in_2, w_ffn_out_2,
):
    x = first_block(
        x, c, w_in, w_out, sinks, rel_bias, w_ada, b_ada, norm_gains, w1, b1, w2, b2,
    )
    return second_block(
        x, norm_mix_g_2, w_in_2, w_conv_2, w_spatial_2, b_spatial_2, gmlp_ln_g_2, gmlp_ln_b_2,
        fox_q_norm_g_2, fox_k_norm_g_2, fox_forget_b_2, w_branch_2, w_out_2, norm_ffn_g_2,
        w_ffn_in_2, w_ffn_out_2,
    )


_drawn_inputs = setup_inputs


def setup_inputs(seed=0):
    import zlib

    import numpy as np

    out = dict(_drawn_inputs(seed))
    spreads = {}
    factors = {'sinks': 6.327,
     'b1': 5.465,
     'b2': 8.0,
     'gmlp_ln_g_2': 6.344,
     'gmlp_ln_b_2': 26.21,
     'fox_q_norm_g_2': 8.0,
     'fox_k_norm_g_2': 8.0,
     'b_spatial_2': 3.483,
     'norm_ffn_g_2': 3.115}
    for name, (base, spread) in spreads.items():
        noise = np.random.default_rng([zlib.crc32(name.encode()), seed]).standard_normal(out[name].shape)
        drawn = base * np.exp(spread * noise) if base else spread * noise
        out[name] = __import__('jax').numpy.asarray(drawn.astype(out[name].dtype))
    for name, factor in factors.items():
        out[name] = (out[name] * factor).astype(out[name].dtype)
    return out
```

```python
import numpy as np

import concourse.bass as bass
from concourse import mybir
from contextlib import ExitStack

P = 128
ROWS = 256
RT = ROWS // P
D = 1024
KT = D // P
HD = 64
SCALE = HD ** -0.5
EPS = 1e-6
NEG = -1e30
BIG = 3e38
N_HEADS = 16
N_MOBA = 8
N_KV = 2
WINDOW = 128
N_BUCKETS = 32
MAX_DISTANCE = 128
W_A = N_MOBA * HD
W_KV = N_KV * HD
D_IN = 3 * W_A + (N_HEADS - N_MOBA) * HD + 2 * W_KV
D_FF = 4 * D
MIX = 256
FF2 = 2816
N_BRANCH = 4
GATE0 = 6 * MIX + 2 * MIX + 2 * MIX + 4 + 0
UNIT = 1024
RING = 4
AHEAD = 3
DIST = 384
WMASK_ROW = 64
COPIES = 16

C_CB, C_CC, C_CX, C_UV = 0, MIX, 2 * MIX, 3 * MIX
C_SBQ, C_SBK, C_SBV = 5 * MIX, 6 * MIX, 7 * MIX
C_FXQ, C_FXK, C_FXV, C_F = 8 * MIX, 9 * MIX, 10 * MIX, 11 * MIX
C_GATE = C_F + 4

V_NG, V_B1, V_NMIX, V_NFFN, V_CONV, V_C, V_GQ, V_GK, V_BSP = 0, 32, 64, 72, 80, 86, 94, 95, 96
V_ROWS = 100
ADA_ROWS = 6 * D // P
M_SH1, M_SC1, M_G1, M_SH2, M_SC2, M_G2 = 0, 8, 16, 24, 32, 40

U_PROJ1 = 0
U_OUT1 = U_PROJ1 + D_IN // P
U_UP1 = U_OUT1 + KT
U_DOWN1 = U_UP1 + D_FF // P
U_PROJ2 = U_DOWN1 + D_FF // P
U_GB = U_PROJ2 + 22
U_OUT2 = U_GB + N_BRANCH * (KT + 2)
U_UP2 = U_OUT2 + KT
U_DOWN2 = U_UP2 + 2 * FF2 // P
U_END = U_DOWN2 + FF2 // P
ADA_FIRST = 16
ADA_UNITS = 48


def raw_index(u):
    return u + (ADA_FIRST if u < U_OUT1 else ADA_UNITS)


ROWS_OUT1, ROWS_DOWN1, ROWS_GATE0, ROWS_OUT2, ROWS_DOWN2 = 0, 1, 2, 10, 11

F_PROJ1 = 15
F_UP1 = F_PROJ1 + D_FF // P
F_PROJ2 = F_UP1 + 14

N_IN1, N_Y1, N_FF1, N_Y2, N_MIX, N_FF2 = range(6)
X_PROJ1, X_UP1, X_PROJ2, X_OUT2, X_UP2 = range(5)

GB_STEPS = {
    0: [("GMIX", 0)], 2: [("GT", 0)], 3: [("CUM", 0)], 4: [("FTQ", 0)], 5: [("FTK", 0)],
}
for _h in range(4):
    GB_STEPS.setdefault(6 + 3 * _h, []).append(("Z", _h))
    GB_STEPS.setdefault(8 + 3 * _h, []).append(("ARG", _h))
    GB_STEPS.setdefault(10 + 3 * _h, []).append(("PVS", _h))
    GB_STEPS.setdefault(20 + 3 * _h, []).append(("QK", 16 + _h))
    GB_STEPS.setdefault(22 + 3 * _h, []).append(("TR", 16 + _h))
    GB_STEPS.setdefault(24 + 3 * _h, []).append(("PV", 16 + _h))


def build_program(nc, a):
    f32, f32r = mybir.dt.float32, mybir.dt.float32r
    ACT = mybir.ActivationFunctionType
    ALU = mybir.AluOpType
    AX = mybir.AxisListType

    w_in = a["w_in"][0].rearrange("(t p) n -> p t n", p=P)
    w_out = a["w_out"][0]
    w1 = a["w1"][0].rearrange("(t p) n -> p t n", p=P)
    w2 = a["w2"][0]
    w_ada = a["w_ada"][0].rearrange("(t p) n -> p t n", p=P)
    w_in2 = a["w_in_2"][0].rearrange("(t p) n -> p t n", p=P)
    w_in2_rows = a["w_in_2"][0]
    w_branch = a["w_branch_2"][0]
    w_out2 = a["w_out_2"][0]
    w_up2 = a["w_ffn_in_2"][0].rearrange("(t p) n -> p t n", p=P)
    w_down2 = a["w_ffn_out_2"][0]
    x_dram = a["x"][0].rearrange("(r p) n -> p r n", p=P)
    out_dram = a["out"][0].rearrange("(r p) n -> p r n", p=P)
    bias_dram = nc.dram_tensor("bias_by_distance", [N_HEADS, COPIES, DIST], f32, kind="Internal").ap()

    ctx = ExitStack()
    with ctx:
        def sb(name, shape, dt=f32, scope=ctx):
            return scope.enter_context(nc.sbuf_tensor(name, shape, dt))

        def sem(name):
            return ctx.enter_context(nc.semaphore(name))

        raw = sb("raw", [P, RING, UNIT])
        wh = sb("wh", [P, RING, UNIT], f32r)
        wl = sb("wl", [P, RING, UNIT], f32r)
        x = sb("x_rows", [P, RT, D])
        xr = sb("rows_tmp", [P, RT, D])
        xT = sb("xT", [P, KT, 2 * ROWS], f32r)
        tmpT = sb("tmpT", [P, 4, ROWS])
        act_t = sb("act_t", [P, 4, ROWS])
        val_t = sb("val_t", [P, 4, ROWS])
        vrows = sb("vrows", [V_ROWS, P])
        arows = sb("arows", [ADA_ROWS, P])
        vT = sb("vT", [P, V_ROWS])
        badaT = sb("badaT", [P, ADA_ROWS])
        cT = sb("cT", [P, KT])
        modT = sb("modT", [P, ADA_ROWS])
        modrow = sb("modrow", [1, 2 * 512])
        A1 = sb("A1", [P, KT])
        A2 = sb("A2", [P, KT])
        gT = sb("gT", [P, 2, KT])
        G1 = sb("G1", [P, D])
        G2 = sb("G2", [P, D])
        b2row = sb("b2row", [1, D])
        ident = sb("ident", [P, P])
        ones = sb("ones", [P, P])
        neg_ge = sb("neg_ge", [P, P])
        neg_ones = sb("neg_ones", [P, P])
        upper = sb("upper", [P, 3 * P])
        causal = sb("causal", [P, ROWS])
        mhalf = sb("mhalf", [P, 16])
        big = sb("big", [P, 1])
        relw = sb("relw", [WMASK_ROW + 1, N_HEADS])
        onehot = sb("onehot", [WMASK_ROW + 1, DIST])
        dist_rows = sb("dist_rows", [N_HEADS, DIST])
        sinks = sb("sinks_b", [P, 8])
        nsink = sb("nsink", [P, 8])
        bf = sb("bf_b", [P, 4])
        lng = sb("lng_b", [P, MIX])
        lnb = sb("lnb_b", [P, MIX])
        wsp = sb("wsp", [P, 4, P])
        wspT = sb("wspT", [P, 4, P])
        wf = sb("wf", [P, KT, 4])
        wfh = sb("wfh", [P, KT, 4], f32r)
        wfl = sb("wfl", [P, KT, 4], f32r)
        ss = sb("ss", [P, 6, RT, 2])
        ms = sb("ms", [P, 6, RT])
        rstd = sb("rstd", [P, 6, RT])
        logits = sb("logits", [P, 2, 386])
        probs = sb("probs", [P, 2, 386])
        probsT = sb("probsT", [P, 2, 384])
        nmax = sb("nmax", [P, 20, RT])
        lsum = sb("lsum", [P, 20, RT])
        rsum = sb("rsum", [P, 20, RT])
        fraw = sb("fraw", [P, RT, 4])
        ft = sb("ft", [P, RT, 4])
        logf = sb("logf", [P, RT, 4])
        bnst = sb("bnst", [P, RT, 6])
        bnag = sb("bnag", [P, RT, 2])
        ln_ms = sb("ln_ms", [P, RT])
        ln_rstd = sb("ln_rstd", [P, RT])
        fx_ss = sb("fx_ss", [P, RT, 8])
        fx_ms = sb("fx_ms", [P, RT, 8])
        fx_rstd = sb("fx_rstd", [P, RT, 8])
        gqs = sb("gqs", [P, 1])
        with ExitStack() as s1:
            hid = sb("hid", [P, D_FF // P, 2 * ROWS], f32r, s1)
        with ExitStack() as s2:
            qT = sb("qT", [P, 8, ROWS], f32, s2)
            kT = sb("kT", [P, 6, ROWS], f32, s2)
            vall = sb("vall", [P, RT, W_A + W_KV], f32, s2)
            dbias = sb("dbias", [P, N_HEADS, ROWS], f32, s2)
        with ExitStack() as s3:
            yT = sb("yT", [P, 8, 2 * ROWS], f32r, s3)
            sig = sb("sig", [P, RT, D], f32, s3)
            gu = sb("gu", [P, RT, 2 * MIX], f32, s3)
            vn = sb("vn", [P, RT, MIX], f32, s3)
            yb = sb("yb", [P, RT, MIX], f32, s3)
            svq = sb("svq", [P, RT, 512], f32, s3)
            fkv = sb("fkv", [P, RT, 512], f32, s3)
            fsq = sb("fsq", [P, 512], f32, s3)
            sbT = sb("sbT", [P, 4, ROWS], f32, s3)
            cbc = sb("cbc", [P, 4, ROWS], f32, s3)
            xcp = sb("xcp", [P, 2, ROWS + 2], f32, s3)
            fT = sb("fT", [P, 4, ROWS], f32, s3)
        merged = xr
        cum, ncum = modrow, b2row

        acc = [ctx.enter_context(nc.psum_tensor(f"acc{i}", [P, 512], f32)) for i in range(4)]
        aux = [ctx.enter_context(nc.psum_tensor(f"aux{i}", [P, 512], f32)) for i in range(4)]

        raw_full = [sem(f"raw_full{i}") for i in range(RING)]
        rounded, split_ready, unit_done, rows_ready = sem("rounded"), sem("split_ready"), sem("unit_done"), sem("rows_ready")
        acc_free = sem("acc_free")
        ada_used, modrow_ready, mod_cols, mod_ready = sem("ada_used"), sem("modrow_ready"), sem("mod_cols"), sem("mod_ready")
        x_loaded, vec_loaded, misc_loaded, bias_loaded = sem("x_loaded"), sem("vec_loaded"), sem("misc_loaded"), sem("bias_loaded")
        consts_made, relw_zeroed, relw_made = sem("consts_made"), sem("relw_zeroed"), sem("relw_made")
        vec_cols, vec_ready, c_ready = sem("vec_cols"), sem("vec_ready"), sem("c_ready")
        dist_done, dist_copied, dist_stored = sem("dist_done"), sem("dist_copied"), sem("dist_stored")
        ss_ready, rstd_ready, normed, resid = sem("ss_ready"), sem("rstd_ready"), sem("normed"), sem("resid")
        nt_ready, tmpT_done, xT_ready = sem("nt_ready"), sem("tmpT_done"), sem("xT_ready")
        scores, scored, exped, p_scaled = sem("scores"), sem("scored"), sem("exped"), sem("p_scaled")
        pt_psum, pt_copied, pv_done, mix_ready = sem("pt_psum"), sem("pt_copied"), sem("pv_done"), sem("mix_ready")
        nsink_made, sink_filled = sem("nsink_made"), sem("sink_filled")
        g_diag, g_psum, g_ready = sem("g_diag"), sem("g_psum"), sem("g_ready")
        hid_hi, hid_sq, hid_ready, silu_done = sem("hid_hi"), sem("hid_sq"), sem("hid_ready"), sem("silu_done")
        sig_done, branch_done = sem("sig_done"), sem("branch_done")
        wf_split, f_psum, f_added, f_abs, f_e, f_l, logf_ready = (sem(n) for n in ("wf_split", "f_psum", "f_added", "f_abs", "f_e", "f_l", "logf_ready"))
        cum_psum, cum_ready = sem("cum_psum"), sem("cum_ready")
        ws_psum, ws_copied, ws_ready = sem("ws_psum"), sem("ws_copied"), sem("ws_ready")
        ln_stat, ln_rstd_ready, vn_ready, gmix_done, yb_ready, yb_psum = (sem(n) for n in ("ln_stat", "ln_rstd_ready", "vn_ready", "gmix_done", "yb_ready", "yb_psum"))
        y_ready = sem("y_ready")
        xc_ready, conv_ready = sem("xc_ready"), sem("conv_ready")
        fx_stat, fx_rstd_ready, fx_normed, fx_psum, fxT_ready = (sem(n) for n in ("fx_stat", "fx_rstd_ready", "fx_normed", "fx_psum", "fxT_ready"))
        z_psum, z_abs, z_exp, z_ln, sp_made, sp_masked = (sem(n) for n in ("z_psum", "z_abs", "z_exp", "z_ln", "sp_made", "sp_masked"))
        arg_psum, w_exped, w_masked, pvs_done, sb_ready, fox_ready = (sem(n) for n in ("arg_psum", "w_exped", "w_masked", "pvs_done", "sb_ready", "fox_ready"))
        act_step, dve_step, pool_step = sem("act_step"), sem("dve_step"), sem("pool_step")
        out_done = sem("out_done")

        block = ctx.enter_context(nc.Block())

        def slot_of(u):
            return u % RING

        def col_src(w, col):
            return w[:, :, col:col + P]

        def proj1_col(k):
            if k < 8:
                return k * P
            if 12 <= k < 16:
                return 3 * W_A + (k - 12) * P
            return 3 * W_A + 512 + (k - 16) * P

        PROJ2 = ([("narrow", C_UV, g) for g in range(4)]
                 + [("col", C_SBQ + P * i, 0) for i in range(4)]
                 + [("narrow", C_SBV, g) for g in range(4)]
                 + [("narrow", C_FXK, g) for g in range(4)]
                 + [("col", C_CB + P * i, 0) for i in range(6)])

        @block.sync
        def _(sp):
            def full(k):
                return raw_full[k % RING]

            def slot8(k):
                return raw[:, k % RING, :].rearrange("p (t n) -> p t n", t=KT)

            def slot2(k):
                return raw[:, k % RING, :].rearrange("p (t n) -> p t n", t=2)

            def ada(i):
                v = i if i < ADA_FIRST else i + U_OUT1
                if i >= RING and not ADA_FIRST <= i < ADA_FIRST + RING:
                    sp.wait_ge(ada_used, i - RING + 1)
                elif i >= ADA_FIRST:
                    sp.wait_ge(split_ready, v - RING - ADA_FIRST + 1)
                j, g = divmod(i, 4)
                sp.dma_start(slot2(v), w_ada[:, 2 * g:2 * g + 2, 512 * j:512 * (j + 1)]).then_inc(full(v), 16)

            def free(u):
                sp.wait_ge(split_ready, u - RING + 1)

            sp.dma_start(x[:, :, :], x_dram).then_inc(x_loaded, 16)
            for i in range(ADA_FIRST):
                ada(i)
            for k in range(U_OUT1):
                if k < RING:
                    sp.wait_ge(ada_used, ADA_FIRST - RING + k + 1)
                else:
                    free(k)
                if 8 <= k < 12:
                    sp.dma_start(slot2(k), w_in[:, 2 * (k - 8):2 * (k - 8) + 2, 2 * W_A:3 * W_A]).then_inc(full(k), 16)
                else:
                    sp.dma_start(slot8(k), col_src(w_in, proj1_col(k))).then_inc(full(k), 16)
                if k == 7:
                    sp.wait_ge(dist_stored, 16)
                    for g in range(P // COPIES):
                        sp.dma_start(dbias[COPIES * g:COPIES * (g + 1), :, :],
                                     bass.AP(tensor=bias_dram.tensor, offset=P - 1 - COPIES * g,
                                             ap=[[DIST - 1, COPIES], [COPIES * DIST, N_HEADS], [1, ROWS]])).then_inc(bias_loaded, 16)
            for i in range(ADA_FIRST, ADA_UNITS):
                ada(i)
            for k in range(KT):
                if k < RING:
                    sp.wait_ge(ada_used, ADA_UNITS - RING + k + 1)
                else:
                    free(U_OUT1 + k)
                sp.dma_start(raw[:, slot_of(U_OUT1 + k), :], w_out[P * k:P * (k + 1), :]).then_inc(full(U_OUT1 + k), 16)
            with sp.Fori(0, D_FF // P // RING) as i:
                for k in range(RING):
                    free(U_UP1 + RING * i + k)
                    sp.dma_start(slot8(U_UP1 + k), w1[:, :, bass.ds(RING * P * i + P * k, P)]).then_inc(full(U_UP1 + k), 16)
            with sp.Fori(0, D_FF // P // RING) as i:
                for k in range(RING):
                    free(U_DOWN1 + RING * i + k)
                    sp.dma_start(raw[:, slot_of(U_DOWN1 + k), :], w2[bass.ds(RING * P * i + P * k, P), :])\
                        .then_inc(full(U_DOWN1 + k), 16)
            for k, (form, col, g) in enumerate(PROJ2):
                free(U_PROJ2 + k)
                if form == "narrow":
                    sp.dma_start(slot2(U_PROJ2 + k), w_in2[:, 2 * g:2 * g + 2, col:col + 512]).then_inc(full(U_PROJ2 + k), 16)
                else:
                    sp.dma_start(slot8(U_PROJ2 + k), col_src(w_in2, col)).then_inc(full(U_PROJ2 + k), 16)
            for n in range(N_BRANCH):
                u0 = U_GB + n * (KT + 2)
                for k in range(KT + 2):
                    free(u0 + k)
                    if k < KT:
                        src = w_in2_rows[P * k:P * (k + 1), C_GATE + D * n:C_GATE + D * (n + 1)]
                    else:
                        src = w_branch[n, P * (k - KT):P * (k - KT + 1), :]
                    sp.dma_start(raw[:, slot_of(u0 + k), :], src).then_inc(full(u0 + k), 16)
            for k in range(KT):
                free(U_OUT2 + k)
                sp.dma_start(raw[:, slot_of(U_OUT2 + k), :], w_out2[P * k:P * (k + 1), :]).then_inc(full(U_OUT2 + k), 16)
            with sp.Fori(0, FF2 // P // 2) as i:
                for k in range(RING):
                    free(U_UP2 + RING * i + k)
                    sp.dma_start(slot8(U_UP2 + k), w_up2[:, :, bass.ds(2 * P * i + FF2 * (k % 2) + P * (k // 2), P)])\
                        .then_inc(full(U_UP2 + k), 16)
            for k in range(FF2 // P):
                free(U_DOWN2 + k)
                sp.dma_start(raw[:, slot_of(U_DOWN2 + k), :], w_down2[P * k:P * (k + 1), :]).then_inc(full(U_DOWN2 + k), 16)
            for r in range(RT):
                sp.wait_ge(resid, 6 + r + 1)
                sp.dma_start(out_dram[:, r, :], x[:, r, :]).then_inc(out_done, 16)
            sp.wait_ge(out_done, 16 * RT)

        @block.gpsimd
        def _(pool):
            steps = [0]

            def link(ins):
                steps[0] += 1
                ins.then_inc(pool_step, 1)
                pool.wait_ge(pool_step, steps[0])

            def rsqrt(out, tmp, in_, scale, n, done):
                link(nc.gpsimd.tensor_scalar(tmp, in_, scale, EPS, ALU.mult, ALU.add))
                nc.gpsimd.tensor_tensor(out, tmp, mhalf[:, 0:n], ALU.pow).then_inc(done, 1)

            nc.gpsimd.memset(relw[:, :], 0.0).then_inc(relw_zeroed, 1)
            pool.wait_ge(relw_zeroed, 1)
            nc.gpsimd.memset(relw[N_BUCKETS:N_BUCKETS + 1, :], 1.0).then_inc(relw_made, 1)
            pool.wait_ge(relw_made, 1)
            nc.gpsimd.memset(relw[WMASK_ROW:WMASK_ROW + 1, N_MOBA:], 1.0).then_inc(relw_made, 1)
            pool.wait_ge(relw_made, 2)
            nc.gpsimd.memset(ident[:, :], 0.0)
            nc.gpsimd.memset(ones[:, :], 1.0)
            nc.gpsimd.memset(neg_ones[:, :], -1.0)
            nc.gpsimd.memset(neg_ge[:, :], -1.0)
            nc.gpsimd.memset(upper[:, :], 1.0)
            nc.gpsimd.memset(causal[:, :], 0.0)
            nc.gpsimd.memset(big[:, :], BIG)
            link(nc.gpsimd.memset(mhalf[:, :], -0.5))
            nc.gpsimd.affine_select(out=ident[:, :], in_=ident[:, :], compare_op=ALU.not_equal, fill=1.0, base=0,
                                    pattern=[[-1, P]], channel_multiplier=1).then_inc(consts_made, 1)
            nc.gpsimd.affine_select(out=neg_ge[:, :], in_=neg_ge[:, :], compare_op=ALU.is_ge, fill=0.0, base=0,
                                    pattern=[[-1, P]], channel_multiplier=1).then_inc(consts_made, 1)
            nc.gpsimd.affine_select(out=upper[:, :], in_=upper[:, :], compare_op=ALU.is_ge, fill=0.0, base=-P,
                                    pattern=[[1, 3 * P]], channel_multiplier=-1).then_inc(consts_made, 1)
            nc.gpsimd.affine_select(out=causal[:, :], in_=causal[:, :], compare_op=ALU.is_ge, fill=NEG, base=P,
                                    pattern=[[-1, ROWS]], channel_multiplier=1).then_inc(consts_made, 1)

            def norm_rstd(n, parts):
                for r in range(RT):
                    pool.wait_ge(ss_ready, RT * n + r + 1)
                    if parts == 2:
                        link(nc.gpsimd.tensor_tensor(ss[:, n, r, 0:1], ss[:, n, r, 0:1], ss[:, n, r, 1:2], ALU.add))
                    rsqrt(rstd[:, n, r:r + 1], ms[:, n, r:r + 1], ss[:, n, r, 0:1], 1.0 / D, 1, rstd_ready)

            norm_rstd(N_IN1, 1)
            pool.wait_ge(misc_loaded, 16 * 9)
            nc.gpsimd.tensor_scalar(nsink[:, :], sinks[:, :], -1.0, None, ALU.mult).then_inc(nsink_made, 1)
            pool.wait_ge(nsink_made, 1)
            for h in range(N_MOBA, N_HEADS):
                pool.wait_ge(exped, 2 * (h - 1))
                nc.gpsimd.tensor_copy(logits[:, h % 2, 128:386:257], nsink[:, h - N_MOBA:h - N_MOBA + 1].to_broadcast([P, 2]))\
                    .then_inc(sink_filled, 1)
            norm_rstd(N_Y1, 2)
            norm_rstd(N_FF1, 1)
            norm_rstd(N_Y2, 2)
            pool.wait_ge(ws_copied, 1)
            nc.gpsimd.affine_select(out=wspT[:, :, :], in_=wspT[:, :, :], compare_op=ALU.is_ge, fill=0.0, base=0,
                                    pattern=[[0, 4], [1, P]], channel_multiplier=-1).then_inc(ws_ready, 1)
            norm_rstd(N_MIX, 1)
            for r in range(RT):
                pool.wait_ge(ln_stat, r + 1)
                rsqrt(ln_rstd[:, r:r + 1], ln_ms[:, r:r + 1], bnag[:, r, 1:2], 1.0, 1, ln_rstd_ready)
            for r in range(RT):
                pool.wait_ge(fx_stat, 2 * (r + 1))
                rsqrt(fx_rstd[:, r, :], fx_ms[:, r, :], fx_ss[:, r, :], 1.0 / HD, 8, fx_rstd_ready)
            for h in range(4):
                pool.wait_ge(sp_made, h + 1)
                diag = probs[:, 0, 0:384].rearrange("p (b q) -> p b q", b=3)[:, 0:3:2, :]
                nc.gpsimd.affine_select(out=diag, in_=diag, compare_op=ALU.is_gt, fill=0.0, base=0,
                                        pattern=[[0, 2], [1, P]], channel_multiplier=-1).then_inc(sp_masked, 1)
                pool.wait_ge(w_exped, h + 1)
                diag = probsT[:, 0, :].rearrange("p (b q) -> p b q", b=3)[:, 0:3:2, :]
                nc.gpsimd.affine_select(out=diag, in_=diag, compare_op=ALU.is_gt, fill=0.0, base=0,
                                        pattern=[[0, 2], [1, P]], channel_multiplier=-1).then_inc(w_masked, 1)
            norm_rstd(N_FF2, 1)

        @block.scalar
        def _(act):
            A = nc.scalar.activation

            def round_unit(u, wait_full, wait_free, s):
                act.wait_ge(raw_full[s], wait_full)
                if wait_free is not None:
                    act.wait_ge(unit_done, wait_free)
                A(wh[:, s, :], raw[:, s, :], ACT.Copy).then_inc(rounded, 1)

            def round_static(u):
                if u < U_END:
                    round_unit(u, 16 * (raw_index(u) // RING + 1), u - RING + 1 if u >= RING else None, slot_of(u))

            def round_looped(u0, i, k):
                s = slot_of(u0 + k)
                round_unit(None, 16 * ((u0 + k + ADA_UNITS) // RING + 1) + 16 * i, u0 + k - RING + 1 + RING * i, s)

            def squares(n, r):
                A(xr[:, r, :], x[:, r, :], ACT.Square, accum_out=ss[:, n, r, 0:1]).then_inc(ss_ready, 1)

            def squares_acc(n, rows, u_last):
                for r in range(RT):
                    for c in range(2):
                        g = 2 * r + c
                        if g < 3:
                            act.wait_ge(rows_ready, 3 * rows + g + 1)
                        else:
                            act.wait_ge(unit_done, u_last + 1)
                        ins = A(xr[:, r, 512 * c:512 * (c + 1)], acc[g][:, :], ACT.Square, accum_out=ss[:, n, r, c:c + 1])
                    ins.then_inc(ss_ready, 1)

            def from_transposed(t, scale, bias):
                for kt in range(KT):
                    if kt % 2 == 0:
                        act.wait_ge(nt_ready, 4 * t + kt // 2 + 1)
                    if KT * t + kt >= 4:
                        act.wait_ge(xT_ready, KT * t + kt - 3)
                    src = aux[kt // 2][:, ROWS * (kt % 2):ROWS * (kt % 2) + ROWS]
                    kw = {} if bias is None else {"bias": bias[:, kt:kt + 1]}
                    if scale is not None:
                        kw["scale"] = scale[:, kt:kt + 1]
                    A(tmpT[:, kt % 4, :], src, ACT.Identity if kw else ACT.Copy, **kw).then_inc(tmpT_done, 1)

            vec = [(vrows[V_NG:V_NG + 32, :], a["norm_gains"][0].rearrange("g (t p) -> (g t) p", p=P)),
                   (vrows[V_B1:V_B1 + 32, :], a["b1"][0].rearrange("(t p) -> t p", p=P)),
                   (vrows[V_NMIX:V_NMIX + 8, :], a["norm_mix_g_2"][0].rearrange("(t p) -> t p", p=P)),
                   (vrows[V_NFFN:V_NFFN + 8, :], a["norm_ffn_g_2"][0].rearrange("(t p) -> t p", p=P)),
                   (vrows[V_CONV:V_CONV + 6, :], a["w_conv_2"][0].rearrange("j (t p) -> (j t) p", p=P)),
                   (vrows[V_C:V_C + 8, :], a["c"][0].rearrange("(t p) -> t p", p=P)),
                   (vrows[V_BSP:V_BSP + 4, :], a["b_spatial_2"][0]),
                   (arows[:, :], a["b_ada"][0].rearrange("(t p) -> t p", p=P))]
            for half in range(2):
                vec.append((vrows[V_GQ:V_GQ + 1, HD * half:HD * (half + 1)], a["fox_q_norm_g_2"]))
                vec.append((vrows[V_GK:V_GK + 1, HD * half:HD * (half + 1)], a["fox_k_norm_g_2"]))
            for dst, src in vec:
                act.dma_start(dst, src).then_inc(vec_loaded, 16)
            n_vec = len(vec)
            act.wait_ge(relw_made, 2)
            for dst, src in [
                (relw[0:N_BUCKETS, :], a["rel_bias"]),
                (onehot[:, :], a["bucket_onehot"]),
                (sinks[:, :], a["sinks"][0].partition_broadcast(P)),
                (bf[:, :], a["fox_forget_b_2"][0].partition_broadcast(P)),
                (lng[:, :], a["gmlp_ln_g_2"][0].partition_broadcast(P)),
                (lnb[:, :], a["gmlp_ln_b_2"][0].partition_broadcast(P)),
                (b2row[:, :], a["b2"]),
                (wsp[:, :, :], a["w_spatial_2"][0].rearrange("g t s -> t g s")),
                (wf[:, :, :], w_in2[:, :, C_F:C_F + 4]),
            ]:
                act.dma_start(dst, src).then_inc(misc_loaded, 16)

            act.wait_ge(x_loaded, 16)
            for r in range(RT):
                squares(N_IN1, r)
            act.wait_ge(vec_ready, 2)
            A(cT[:, :], vT[:, V_C:V_C + KT], ACT.Silu).then_inc(c_ready, 1)
            for u in range(AHEAD):
                round_static(u)
            act.wait_ge(dist_copied, 1)
            act.dma_start(bias_dram, dist_rows[:, :].unsqueeze(1).to_broadcast([N_HEADS, COPIES, DIST])).then_inc(dist_stored, 16)
            act.wait_ge(mod_ready, 1)
            from_transposed(X_PROJ1, A1, modT[:, M_SH1:M_SH1 + KT])
            for k in range(U_OUT1):
                if k + AHEAD < U_OUT1:
                    round_static(k + AHEAD)
                act.wait_ge(unit_done, k + 1)
                bank = acc[k % 4]
                if k < 4:
                    A(qT[:, k, :], bank[:, 0:ROWS], ACT.Copy, scale=SCALE).then_inc(acc_free, 1)
                elif k < 8:
                    A(kT[:, k - 4, :], bank[:, 0:ROWS], ACT.Copy).then_inc(acc_free, 1)
                elif k == 11:
                    A(vall[:, 0, 0:W_A], acc[0][:, :], ACT.Copy)
                    A(vall[:, 1, 0:W_A], acc[1][:, :], ACT.Copy).then_inc(acc_free, 1)
                elif 12 <= k < 16:
                    A(qT[:, k - 8, :], bank[:, 0:ROWS], ACT.Copy, scale=SCALE).then_inc(acc_free, 1)
                elif k == 16:
                    for kv in range(N_KV):
                        for half in range(2):
                            ins = A(kT[HD * half:HD * (half + 1), 4 + kv, :], bank[HD * kv:HD * (kv + 1), 0:ROWS], ACT.Copy)
                    ins.then_inc(acc_free, 1)
                elif k == 17:
                    A(vall[:, :, W_A:], bank[:, 0:ROWS].rearrange("p (r n) -> p r n", r=RT), ACT.Copy).then_inc(acc_free, 1)

            def exp_head(h):
                for r in range(RT):
                    act.wait_ge(scored, 2 * h + r + 1)
                    lo, n = (0, 128) if r == 0 else (129, 256)
                    if N_MOBA <= h < N_HEADS:
                        if r == 0:
                            act.wait_ge(sink_filled, h - N_MOBA + 1)
                        n += 1
                    if r == 0 and h >= 2:
                        act.wait_ge(pt_psum, h - 1 if h < N_HEADS else h)
                    b = h % 2 if h < N_HEADS else 1
                    A(probs[:, b, lo:lo + n], logits[:, b, lo:lo + n], ACT.Exp, bias=nmax[:, h, r:r + 1], scale=-1.0,
                      accum_out=lsum[:, h, r:r + 1]).then_inc(exped, 1)

            def copy_probsT(h):
                b = h % 2 if h < N_HEADS else 1
                act.wait_ge(pt_psum, h + 1)
                if h >= 2:
                    act.wait_ge(pv_done, h - 1 if h < N_HEADS else h)
                src = aux[2 + h % 2] if h < N_HEADS else aux[1]
                A(probsT[:, b, :], src[:, 0:384], ACT.Copy).then_inc(pt_copied, 1)

            for i in range(N_HEADS + 1):
                if i < N_HEADS:
                    exp_head(i)
                if i >= 1:
                    copy_probsT(i - 1)
            for u in range(U_OUT1, U_OUT1 + AHEAD):
                round_static(u)
            for k in range(KT):
                round_static(U_OUT1 + k + AHEAD)
                if k == 4:
                    for g in range(2):
                        act.wait_ge(g_psum, g + 1)
                        dst = (G1, G2)[g]
                        A(dst[:, 0:512], aux[2 * g][:, :], ACT.Copy)
                        A(dst[:, 512:], aux[2 * g + 1][:, :], ACT.Copy).then_inc(g_ready, 1)
            squares_acc(N_Y1, ROWS_OUT1, U_OUT1 + KT - 1)
            for r in range(RT):
                act.wait_ge(resid, r + 1)
                squares(N_FF1, r)
            from_transposed(X_UP1, A2, modT[:, M_SH2:M_SH2 + KT])
            with act.Fori(0, D_FF // P // RING) as i:
                for k in range(RING):
                    round_looped(U_UP1 + AHEAD, i, k)
                    act.wait_ge(unit_done, U_UP1 + k + 1 + RING * i)
                    act.wait_ge(hid_ready, RING * i + k + 1)
                    A(act_t[:, k, :], acc[k][:, 0:ROWS], ACT.Relu, bias=vT[:, bass.ds(V_B1 + k + RING * i, 1)]).then_inc(acc_free, 1)
                    act.wait_ge(acc_free, F_PROJ1 + k + 1 + RING * i)
                    A(hid[:, RING * i + k, 0:ROWS], act_t[:, k, :], ACT.Square).then_inc(hid_hi, 1)
            with act.Fori(0, D_FF // P // RING) as i:
                for k in range(RING):
                    round_looped(U_DOWN1 + AHEAD, i, k)
            squares_acc(N_Y2, ROWS_DOWN1, U_PROJ2 - 1)
            for r in range(RT):
                act.wait_ge(resid, 2 + r + 1)
                squares(N_MIX, r)
            act.wait_ge(ws_psum, 1)
            A(wspT[:, :, :], aux[0][:, :].rearrange("p (g t) -> p g t", g=4), ACT.Copy).then_inc(ws_copied, 1)
            act.wait_ge(misc_loaded, 16 * 9)
            A(wfh[:, :, :], wf[:, :, :], ACT.Copy).then_inc(wf_split, 1)
            from_transposed(X_PROJ2, vT[:, V_NMIX:V_NMIX + KT], None)
            for k in range(22):
                round_static(U_PROJ2 + k + AHEAD)
                act.wait_ge(unit_done, U_PROJ2 + k + 1)
                if k == 3:
                    for r in range(RT):
                        A(gu[:, r, :], acc[r][:, :], ACT.Gelu_apprx_tanh).then_inc(acc_free, 1)
                elif 4 <= k < 6:
                    A(sbT[:, k - 4, :], acc[k - 2][:, 0:ROWS], ACT.Copy, scale=SCALE).then_inc(acc_free, 1)
                elif 6 <= k < 8:
                    A(sbT[:, k - 4, :], acc[k - 6][:, 0:ROWS], ACT.Copy).then_inc(acc_free, 1)
                elif k == 11:
                    for r in range(RT):
                        A(svq[:, r, :], acc[2 + r][:, :], ACT.Copy).then_inc(acc_free, 1)
                elif k == 15:
                    for r in range(RT):
                        A(fkv[:, r, :], acc[r][:, :], ACT.Copy).then_inc(acc_free, 1)
                elif 16 <= k < 20:
                    A(cbc[:, k - 16, :], acc[(2, 3, 0, 1)[k - 16]][:, 0:ROWS], ACT.Copy).then_inc(acc_free, 1)
            act.wait_ge(f_added, 1)
            A(ft[:, :, :], fraw[:, :, :], ACT.Abs).then_inc(f_abs, 1)
            act.wait_ge(f_abs, 1)
            A(ft[:, :, :], ft[:, :, :], ACT.Exp, scale=-1.0).then_inc(f_e, 1)
            act.wait_ge(f_e, 1)
            A(ft[:, :, :], ft[:, :, :], ACT.Ln, bias=1.0).then_inc(f_l, 1)

            def softplus_parts(h):
                act.wait_ge(z_psum, h + 1)
                buf = logits[:, 0, 0:384]
                if h >= 1:
                    act.wait_ge(sp_made, h)
                A(buf, aux[0][:, 0:384], ACT.Abs).then_inc(z_abs, 1)
                act.wait_ge(z_abs, h + 1)
                A(buf, buf, ACT.Exp, scale=-1.0).then_inc(z_exp, 1)
                act.wait_ge(z_exp, h + 1)
                A(buf, buf, ACT.Ln, bias=1.0).then_inc(z_ln, 1)

            for n in range(N_BRANCH):
                for k in range(KT + 2):
                    i = n * (KT + 2) + k
                    round_static(U_GB + i + AHEAD)
                    if k == KT - 1:
                        for g in range(4):
                            if g < 3:
                                act.wait_ge(rows_ready, 3 * (ROWS_GATE0 + 2 * n) + g + 1)
                            else:
                                act.wait_ge(unit_done, U_GB + i + 1)
                            if n >= 1:
                                act.wait_ge(branch_done, 4 * (n - 1) + g + 1)
                            A(sig[:, g // 2, 512 * (g % 2):512 * (g % 2) + 512], acc[g][:, :], ACT.Sigmoid).then_inc(sig_done, 1)
                    for step, h in GB_STEPS.get(i, []):
                        if step == "CUM":
                            for g in range(2):
                                act.wait_ge(cum_psum, g + 1)
                                A(cum[0:1, 512 * g:512 * (g + 1)], aux[g][0:1, :], ACT.Copy)
                                ins = A(ncum[0:1, 512 * g:512 * (g + 1)], aux[g][0:1, :], ACT.Copy, scale=-1.0)
                            ins.then_inc(cum_ready, 1)
                        elif step == "FTQ" or step == "FTK":
                            s = int(step == "FTK")
                            act.wait_ge(fx_psum, s + 1)
                            gain = (gqs[:, 0:1], vT[:, V_GK:V_GK + 1])[s]
                            A(fT[:, 2 * s:2 * s + 2, :], aux[3 - s][:, :].rearrange("p (t n) -> p t n", t=2), ACT.Identity,
                              scale=gain).then_inc(fxT_ready, 1)
                        elif step == "Z":
                            softplus_parts(h)
                        elif step == "ARG":
                            act.wait_ge(arg_psum, h + 1)
                            if h >= 1:
                                act.wait_ge(pvs_done, h)
                            A(probsT[:, 0, :], aux[1][:, 0:384], ACT.Exp).then_inc(w_exped, 1)
                        elif step == "QK":
                            exp_head(h)
                        elif step == "TR":
                            copy_probsT(h)
            from_transposed(X_OUT2, None, None)
            for k in range(KT):
                round_static(U_OUT2 + k + AHEAD)
            for r in range(RT):
                act.wait_ge(resid, 4 + r + 1)
                squares(N_FF2, r)
            from_transposed(X_UP2, vT[:, V_NFFN:V_NFFN + KT], None)
            with act.Fori(0, FF2 // P // 2) as i:
                for k in range(RING):
                    round_looped(U_UP2 + AHEAD, i, k)
                    if k % 2 == 0:
                        act.wait_ge(unit_done, U_UP2 + k + 1 + RING * i)
                        act.wait_ge(hid_ready, RING + D_FF // P + 2 * i + k // 2 - 1)
                        A(act_t[:, k // 2, :], acc[k][:, 0:ROWS], ACT.Silu).then_inc(silu_done, 1)
            for k in range(FF2 // P):
                round_static(U_DOWN2 + k + AHEAD)

        @block.vector
        def _(dve):
            V = nc.vector
            steps = [0]

            def link(ins):
                steps[0] += 1
                ins.then_inc(dve_step, 1)
                dve.wait_ge(dve_step, steps[0])

            def low_unit(wait, s):
                dve.wait_ge(rounded, wait)
                V.tensor_tensor(wl[:, s, :], raw[:, s, :], wh[:, s, :].bitcast(f32), ALU.subtract).then_inc(split_ready, 1)

            def low_static(u):
                if u < U_END:
                    low_unit(u + 1, slot_of(u))

            def split(dst, src, done):
                link(V.tensor_copy(dst[:, 0:ROWS], src))
                V.tensor_tensor(dst[:, ROWS:], src, dst[:, 0:ROWS].bitcast(f32), ALU.subtract).then_inc(done, 1)

            def normalise(n):
                for r in range(RT):
                    dve.wait_ge(rstd_ready, RT * n + r + 1)
                    V.tensor_scalar(xr[:, r, :], x[:, r, :], rstd[:, n, r:r + 1], None, ALU.mult).then_inc(normed, 1)

            def split_transposed(t):
                for kt in range(KT):
                    dve.wait_ge(tmpT_done, KT * t + kt + 1)
                    split(xT[:, kt, :], tmpT[:, kt % 4, :], xT_ready)

            def gated_residual(n, gain):
                for r in range(RT):
                    dve.wait_ge(rstd_ready, RT * n + r + 1)
                    for c in range(2):
                        ins = V.scalar_tensor_tensor(out=xr[:, r, 512 * c:512 * (c + 1)], in0=acc[2 * r + c][:, :],
                                                     scalar=rstd[:, n, r:r + 1], in1=gain[:, 512 * c:512 * (c + 1)],
                                                     op0=ALU.mult, op1=ALU.mult)
                    link(ins)
                    V.tensor_tensor(x[:, r, :], x[:, r, :], xr[:, r, :], ALU.add).then_inc(resid, 1)

            def plain_residual(rows, u_last):
                for r in range(RT):
                    for c in range(2):
                        g = 2 * r + c
                        if g < 3:
                            dve.wait_ge(rows_ready, 3 * rows + g + 1)
                        else:
                            dve.wait_ge(unit_done, u_last + 1)
                        xs = x[:, r, 512 * c:512 * (c + 1)]
                        ins = V.tensor_tensor(xs, acc[g][:, :], xs, ALU.add)
                    ins.then_inc(resid, 1)

            V.memset(val_t[:, :, :], 0.0).then_inc(hid_ready, RING)
            dve.wait_ge(vec_cols, 1)
            V.tensor_copy(vT[:, :], aux[0][:, 0:V_ROWS]).then_inc(vec_ready, 1)
            V.tensor_copy(badaT[:, :], aux[0][:, P:P + ADA_ROWS]).then_inc(vec_ready, 1)
            normalise(N_IN1)
            dve.wait_ge(dist_done, 1)
            V.tensor_copy(dist_rows[:, :], aux[1][0:N_HEADS, 0:DIST]).then_inc(dist_copied, 1)

            def mod_row(j):
                dve.wait_ge(ada_used, 4 * (j + 1))
                if j >= 2:
                    dve.wait_ge(mod_cols, j - 1)
                V.tensor_copy(modrow[0:1, 512 * (j % 2):512 * (j % 2) + 512], acc[0][0:1, :]).then_inc(modrow_ready, 1)

            for j in range(4):
                mod_row(j)
            dve.wait_ge(mod_cols, 4)
            link(V.tensor_tensor(modT[:, 0:16], acc[1][:, 0:16], badaT[:, 0:16], ALU.add))
            V.scalar_tensor_tensor(out=A1[:, :], in0=modT[:, M_SC1:M_SC1 + KT], scalar=1.0, in1=vT[:, V_NG:V_NG + KT],
                                   op0=ALU.add, op1=ALU.mult).then_inc(mod_ready, 1)
            for u in range(AHEAD):
                low_static(u)
            split_transposed(X_PROJ1)
            for k in range(U_OUT1):
                if k + AHEAD < U_OUT1:
                    low_static(k + AHEAD)

            def score_head(h, bias):
                b = h % 2 if h < N_HEADS else 1
                bank = aux[h % 2] if h < N_HEADS else aux[0]
                first = nsink[:, h - N_MOBA:h - N_MOBA + 1] if N_MOBA <= h < N_HEADS else big[:, 0:1]
                dve.wait_ge(scores, h + 1)
                if h >= 2:
                    dve.wait_ge(exped, 2 * (h - 1) if h < N_HEADS else 2 * h)
                V.tensor_tensor_reduce(out=logits[:, b, 0:128], in0=bank[:, 0:128], in1=bias[:, 128:256], scale=-1.0,
                                       scalar=first, op0=ALU.add, op1=ALU.min, accum_out=nmax[:, h, 0:1]).then_inc(scored, 1)
                V.tensor_tensor_reduce(out=logits[:, b, 129:385], in0=bank[:, 128:384], in1=bias[:, 0:256], scale=-1.0,
                                       scalar=first, op0=ALU.add, op1=ALU.min, accum_out=nmax[:, h, 1:2]).then_inc(scored, 1)

            def scale_head(h):
                b = h % 2 if h < N_HEADS else 1
                dve.wait_ge(exped, 2 * h + 2)
                link(V.reciprocal(rsum[:, h, :], lsum[:, h, :]))
                V.tensor_scalar(probs[:, b, 0:128], probs[:, b, 0:128], rsum[:, h, 0:1], None, ALU.mult)
                V.tensor_scalar(probs[:, b, 129:385], probs[:, b, 129:385], rsum[:, h, 1:2], None, ALU.mult).then_inc(p_scaled, 1)

            dve.wait_ge(bias_loaded, 16 * P // COPIES)
            dve.wait_ge(nsink_made, 1)
            dve.wait_ge(consts_made, 4)
            for i in range(N_HEADS + 3):
                if i < N_HEADS:
                    score_head(i, dbias[:, i, :])
                if 1 <= i <= N_HEADS:
                    scale_head(i - 1)
                if i >= 2 and i % 2 == 0 and 4 + (i - 2) // 2 < 12:
                    mod_row(4 + (i - 2) // 2)
                if i >= 3 and i % 2 == 0:
                    p = (i - 4) // 2
                    dve.wait_ge(pv_done, 2 * p + 2)
                    split(xT[:, p, :], acc[2 + p % 2][:, 0:ROWS], mix_ready)
            dve.wait_ge(mod_cols, 12)
            link(V.tensor_tensor(modT[:, 16:], acc[1][:, 16:ADA_ROWS], badaT[:, 16:], ALU.add))
            V.scalar_tensor_tensor(out=A2[:, :], in0=modT[:, M_SC2:M_SC2 + KT], scalar=1.0,
                                   in1=vT[:, V_NG + 2 * KT:V_NG + 3 * KT], op0=ALU.add, op1=ALU.mult).then_inc(mod_ready, 1)
            V.tensor_tensor(gT[:, 0, :], modT[:, M_G1:M_G1 + KT], vT[:, V_NG + KT:V_NG + 2 * KT], ALU.mult)
            link(V.tensor_tensor(gT[:, 1, :], modT[:, M_G2:M_G2 + KT], vT[:, V_NG + 3 * KT:V_NG + 4 * KT], ALU.mult))
            for u in range(U_OUT1, U_OUT1 + AHEAD):
                low_static(u)
            for g in range(2):
                V.tensor_tensor(xr[:, g, :].rearrange("p (t n) -> p t n", t=KT),
                                ident[:, :].unsqueeze(1).to_broadcast([P, KT, P]),
                                gT[:, g, :].unsqueeze(2).to_broadcast([P, KT, P]), ALU.mult).then_inc(g_diag, 1)
            for k in range(KT):
                low_static(U_OUT1 + k + AHEAD)
            dve.wait_ge(g_ready, 1)
            gated_residual(N_Y1, G1)
            normalise(N_FF1)
            split_transposed(X_UP1)
            with dve.Fori(0, D_FF // P // RING) as i:
                for k in range(RING):
                    low_unit(U_UP1 + AHEAD + k + 1 + RING * i, slot_of(U_UP1 + AHEAD + k))
                    dve.wait_ge(acc_free, F_PROJ1 + k + 1 + RING * i)
                    V.tensor_tensor(val_t[:, k, :], act_t[:, k, :], act_t[:, k, :], ALU.mult).then_inc(hid_sq, 1)
                    dve.wait_ge(hid_sq, RING * i + k + 1)
                    dve.wait_ge(hid_hi, RING * i + k + 1)
                    V.tensor_tensor(hid[:, RING * i + k, ROWS:], val_t[:, k, :], hid[:, RING * i + k, 0:ROWS].bitcast(f32),
                                    ALU.subtract).then_inc(hid_ready, 1)
            with dve.Fori(0, D_FF // P // RING) as i:
                for k in range(RING):
                    low_unit(U_DOWN1 + AHEAD + k + 1 + RING * i, slot_of(U_DOWN1 + AHEAD + k))
            dve.wait_ge(g_ready, 2)
            gated_residual(N_Y2, G2)
            normalise(N_MIX)
            dve.wait_ge(wf_split, 1)
            V.tensor_tensor(wfl[:, :, :], wf[:, :, :], wfh[:, :, :].bitcast(f32), ALU.subtract).then_inc(wf_split, 1)
            V.tensor_scalar(gqs[:, :], vT[:, V_GQ:V_GQ + 1], SCALE, None, ALU.mult)
            V.memset(xcp[:, :, 0:2], 0.0)
            split_transposed(X_PROJ2)
            for k in range(22):
                low_static(U_PROJ2 + k + AHEAD)
                if k == 5:
                    for r in range(RT):
                        dve.wait_ge(acc_free, F_UP1 + r + 1)
                        link(V.bn_stats(bnst[:, r, :], gu[:, r, MIX:]))
                        V.bn_aggr(bnag[:, r, :], bnst[:, r, :]).then_inc(ln_stat, 1)
                if k == 7:
                    for r in range(RT):
                        dve.wait_ge(ln_rstd_ready, r + 1)
                        link(V.tensor_scalar(vn[:, r, :], gu[:, r, MIX:], bnag[:, r, 0:1], ln_rstd[:, r:r + 1],
                                             ALU.subtract, ALU.mult))
                        link(V.tensor_tensor(vn[:, r, :], vn[:, r, :], lng[:, :], ALU.mult))
                        V.tensor_tensor(vn[:, r, :], vn[:, r, :], lnb[:, :], ALU.add).then_inc(vn_ready, 1)
                if k == 17:
                    for r in range(RT):
                        dve.wait_ge(acc_free, F_UP1 + 8 + r + 1)
                        for s, src in enumerate((svq[:, r, 256:512], fkv[:, r, 0:256])):
                            link(V.tensor_tensor(fsq[:, 256 * s:256 * (s + 1)], src, src, ALU.mult))
                            V.reduce_sum(fx_ss[:, r, 4 * s:4 * s + 4],
                                         fsq[:, 256 * s:256 * (s + 1)].rearrange("p (h d) -> p h d", h=4), axis=AX.X)\
                                .then_inc(fx_stat, 1)
                if k == 19:
                    for r in range(RT):
                        dve.wait_ge(fx_rstd_ready, r + 1)
                        for s, src in enumerate((svq[:, r, 256:512], fkv[:, r, 0:256])):
                            v = src.rearrange("p (h d) -> p h d", h=4)
                            V.tensor_tensor(v, v, fx_rstd[:, r, 4 * s:4 * s + 4].unsqueeze(2).to_broadcast([P, 4, HD]),
                                            ALU.mult).then_inc(fx_normed, 1)
                if k == 20 or k == 21:
                    t = k - 20
                    dve.wait_ge(unit_done, U_PROJ2 + k + 1)
                    V.tensor_tensor(xcp[:, t, 2:], acc[2 + t][:, 0:ROWS], cbc[:, 2 + t, :], ALU.mult).then_inc(xc_ready, 1)
            dve.wait_ge(f_psum, 1)
            V.tensor_tensor(fraw[:, :, :], aux[3][:, 0:8].rearrange("p (r h) -> p r h", r=RT),
                            bf[:, :].unsqueeze(1).to_broadcast([P, RT, 4]), ALU.add).then_inc(f_added, 1)
            dve.wait_ge(xc_ready, 2)
            for t in range(2):
                wc = [vT[:, V_CONV + 2 * j + t:V_CONV + 2 * j + t + 1] for j in range(3)]
                o = val_t[:, t, :]
                link(V.tensor_scalar(o, xcp[:, t, 2:], wc[2], None, ALU.mult))
                link(V.scalar_tensor_tensor(out=o, in0=xcp[:, t, 1:ROWS + 1], scalar=wc[1], in1=o, op0=ALU.mult, op1=ALU.add))
                link(V.scalar_tensor_tensor(out=o, in0=xcp[:, t, 0:ROWS], scalar=wc[0], in1=o, op0=ALU.mult, op1=ALU.add))
                link(V.tensor_tensor(o, o, cbc[:, t, :], ALU.mult))
                split(yT[:, t, :], o, conv_ready)
            dve.wait_ge(f_l, 1)
            V.scalar_tensor_tensor(out=logf[:, :, :], in0=fraw[:, :, :], scalar=0.0, in1=ft[:, :, :],
                                   op0=ALU.min, op1=ALU.subtract).then_inc(logf_ready, 1)
            for n in range(N_BRANCH):
                for k in range(KT + 2):
                    i = n * (KT + 2) + k
                    low_static(U_GB + i + AHEAD)
                    if k == KT + 1:
                        for g in range(4):
                            if g < 3:
                                dve.wait_ge(rows_ready, 3 * (ROWS_GATE0 + 2 * n + 1) + g + 1)
                            else:
                                dve.wait_ge(unit_done, U_GB + i + 1)
                            cols = slice(512 * (g % 2), 512 * (g % 2) + 512)
                            dst = merged[:, g // 2, cols]
                            if n == 0:
                                V.tensor_tensor(dst, acc[g][:, :], sig[:, g // 2, cols], ALU.mult).then_inc(branch_done, 1)
                            else:
                                s = sig[:, g // 2, cols]
                                link(V.tensor_tensor(s, acc[g][:, :], s, ALU.mult))
                                V.tensor_tensor(dst, dst, s, ALU.add).then_inc(branch_done, 1)
                    for step, h in GB_STEPS.get(i, []):
                        if step == "GMIX":
                            dve.wait_ge(gmix_done, 1)
                            for g in range(4):
                                cols = slice(HD * g, HD * (g + 1))
                                ins = V.scalar_tensor_tensor(out=yb[:, :, cols],
                                                             in0=aux[3][:, P * g:P * (g + 1)].rearrange("p (r e) -> p r e", r=RT),
                                                             scalar=vT[:, V_BSP + g:V_BSP + g + 1], in1=gu[:, :, cols],
                                                             op0=ALU.add, op1=ALU.mult)
                            ins.then_inc(yb_ready, 1)
                        elif step == "GT":
                            dve.wait_ge(yb_psum, 1)
                            for t in range(2):
                                split(yT[:, 2 + t, :], aux[3][:, ROWS * t:ROWS * (t + 1)], y_ready)
                        elif step == "Z":
                            dve.wait_ge(z_ln, h + 1)
                            V.scalar_tensor_tensor(out=probs[:, 0, 0:384], in0=aux[0][:, 0:384], scalar=0.0,
                                                   in1=logits[:, 0, 0:384], op0=ALU.max, op1=ALU.add).then_inc(sp_made, 1)
                        elif step == "PVS" and h % 2 == 1:
                            dve.wait_ge(pvs_done, h + 1)
                            split(yT[:, 4 + h // 2, :], aux[2][:, 0:ROWS], sb_ready)
                        elif step == "QK":
                            score_head(h, causal)
                            scale_head(h)
                        elif step == "PV" and h % 2 == 1:
                            dve.wait_ge(pv_done, h + 1)
                            split(yT[:, 6 + (h - N_HEADS) // 2, :], aux[2][:, 0:ROWS], fox_ready)
            split_transposed(X_OUT2)
            for k in range(KT):
                low_static(U_OUT2 + k + AHEAD)
            plain_residual(ROWS_OUT2, U_UP2 - 1)
            normalise(N_FF2)
            split_transposed(X_UP2)
            with dve.Fori(0, FF2 // P // 2) as i:
                for k in range(RING):
                    low_unit(U_UP2 + AHEAD + k + 1 + RING * i, slot_of(U_UP2 + AHEAD + k))
                    if k % 2 == 1:
                        t = 2 * i + k // 2
                        dve.wait_ge(unit_done, U_UP2 + k + 1 + RING * i)
                        dve.wait_ge(silu_done, t + 1)
                        V.tensor_tensor(val_t[:, k // 2, :], acc[k][:, 0:ROWS], act_t[:, k // 2, :], ALU.mult).then_inc(acc_free, 2)
                        dve.wait_ge(acc_free, F_PROJ2 + 2 * t + 2)
                        V.tensor_copy(hid[:, t, 0:ROWS], val_t[:, k // 2, :]).then_inc(hid_sq, 1)
                        dve.wait_ge(hid_sq, D_FF // P + t + 1)
                        V.tensor_tensor(hid[:, t, ROWS:], val_t[:, k // 2, :], hid[:, t, 0:ROWS].bitcast(f32),
                                        ALU.subtract).then_inc(hid_ready, 1)
            for k in range(FF2 // P):
                low_static(U_DOWN2 + k + AHEAD)
            plain_residual(ROWS_DOWN2, U_END - 1)

        @block.tensor
        def _(pe):
            mm = nc.tensor.matmul

            def transpose(out, in_, n=P):
                return mm(out, in_, ident[0:n, 0:n], start=True, stop=True, is_transpose=True)

            def col_unit(u, wait, bank, moving, waits=None):
                s = slot_of(u)
                pe.wait_ge(split_ready, wait)
                for kt in range(KT):
                    if waits is not None:
                        pe.wait_ge(xT_ready, waits + kt + 1)
                    w = slice(P * kt, P * (kt + 1))
                    hi, lo = moving[:, kt, 0:ROWS], moving[:, kt, ROWS:]
                    mm(bank[:, 0:ROWS], wh[:, s, w], hi, start=(kt == 0), stop=False)
                    mm(bank[:, 0:ROWS], wh[:, s, w], lo, start=False, stop=False)
                    ins = mm(bank[:, 0:ROWS], wl[:, s, w], hi, start=False, stop=(kt == KT - 1))
                ins.then_inc(unit_done, 1)

            def three(bank, still, r, s, cols, first, last):
                hi, lo = still[:, P * r:P * (r + 1)], still[:, ROWS + P * r:ROWS + P * (r + 1)]
                mm(bank, hi, wh[:, s, cols], start=first, stop=False)
                mm(bank, hi, wl[:, s, cols], start=False, stop=False)
                return mm(bank, lo, wh[:, s, cols], start=False, stop=last)

            def narrow_unit(u, g, banks, still):
                s = slot_of(u)
                pe.wait_ge(split_ready, u + 1)
                for r in range(RT):
                    for j in range(2):
                        ins = three(banks[r][:, :], still[:, 2 * g + j, :], r, s, slice(512 * j, 512 * (j + 1)),
                                    g == 0 and j == 0, g == 3 and j == 1)
                ins.then_inc(unit_done, 1)

            def wide_unit(u, still, first, last, bank_wait=None):
                s = slot_of(u)
                pe.wait_ge(split_ready, u + 1)
                for g in range(4):
                    if bank_wait is not None:
                        pe.wait_ge(bank_wait[0], bank_wait[1] + g + 1)
                    ins = three(acc[g][:, :], still, g // 2, s, slice(512 * (g % 2), 512 * (g % 2) + 512), first, last)
                    if last and g < 3:
                        ins.then_inc(rows_ready, 1)
                ins.then_inc(unit_done, 1)

            def to_columns(src, t, wait, base):
                for r in range(RT):
                    pe.wait_ge(wait, base + r + 1)
                    for kt in range(KT):
                        ins = transpose(aux[kt // 2][:, ROWS * (kt % 2) + P * r:ROWS * (kt % 2) + P * (r + 1)],
                                        src[:, r, P * kt:P * (kt + 1)])
                        if r == RT - 1 and kt % 2 == 1:
                            ins.then_inc(nt_ready, 1)

            def ada_unit(i):
                j, g = divmod(i, 4)
                v = i if i < ADA_FIRST else i + U_OUT1
                pe.wait_ge(raw_full[v % RING], 16 * (v // RING + 1))
                if g == 0 and j >= 1:
                    pe.wait_ge(modrow_ready, j)
                for m in range(2):
                    ins = mm(acc[0][0:1, :], cT[:, 2 * g + m:2 * g + m + 1], raw[:, v % RING, 512 * m:512 * (m + 1)],
                             start=(g == 0 and m == 0), stop=(g == 3 and m == 1))
                ins.then_inc(ada_used, 1)

            def mod_columns(j):
                pe.wait_ge(modrow_ready, j + 1)
                for m in range(4):
                    lo = 512 * (j % 2) + P * m
                    ins = mm(acc[1][:, 4 * j + m:4 * j + m + 1], modrow[0:1, lo:lo + P], ones[0:1, 0:1], start=True, stop=True)
                ins.then_inc(mod_cols, 1)

            pe.wait_ge(consts_made, 4)
            pe.wait_ge(vec_loaded, 16 * 12)
            transpose(aux[0][:, 0:V_ROWS], vrows[:, :], V_ROWS)
            transpose(aux[0][:, P:P + ADA_ROWS], arows[:, :], ADA_ROWS).then_inc(vec_cols, 1)
            pe.wait_ge(c_ready, 1)
            for i in range(ADA_FIRST):
                ada_unit(i)
                if i == 1:
                    pe.wait_ge(misc_loaded, 16 * 9)
                    mm(aux[1][0:N_HEADS, 0:DIST], relw[:, :], onehot[:, :], start=True, stop=True).then_inc(dist_done, 1)
                if i == 11:
                    pe.wait_ge(vec_ready, 2)
                    pe.wait_ge(dist_copied, 1)
                    to_columns(xr, X_PROJ1, normed, 0)
                if i % 4 == 1 and i > 4:
                    mod_columns(i // 4 - 1)
            mod_columns(3)
            pe.wait_ge(mod_ready, 1)
            for k in range(U_OUT1):
                if 8 <= k < 12:
                    if k == 8:
                        pe.wait_ge(acc_free, 6)
                    narrow_unit(k, k - 8, acc, xT)
                elif k < 17:
                    if k >= 4:
                        pe.wait_ge(acc_free, k - 3 if k < 8 else (9, 9, 9, 9, 10)[k - 12])
                    col_unit(k, k + 1, acc[k % 4], xT, KT * X_PROJ1 if k == 0 else None)
                else:
                    pe.wait_ge(acc_free, 11)
                    pe.wait_ge(split_ready, k + 1)
                    for r in range(RT):
                        for kt in range(KT):
                            ins = three(acc[k % 4][:, P * r:P * (r + 1)], xT[:, kt, :], r, slot_of(k), slice(P * kt, P * (kt + 1)),
                                        kt == 0, kt == KT - 1)
                    ins.then_inc(unit_done, 1)

            def head_operands(h):
                o = HD * (h % 2)
                if h < N_HEADS:
                    k = kT[o:o + HD, h // 2, :] if h < N_MOBA else kT[o:o + HD, 4 + (h - N_MOBA) // 4, :]
                    vc = HD * h if h < N_MOBA else W_A + HD * ((h - N_MOBA) // 4)
                    return qT[o:o + HD, h // 2, :], k, vall[:, :, vc:vc + HD], aux[h % 2], aux[2 + h % 2], acc[2 + (h // 2) % 2]
                f = h - N_HEADS
                return (fT[o:o + HD, f // 2, :], fT[o:o + HD, 2 + f // 2, :], fkv[:, :, 256 + HD * f:256 + HD * (f + 1)],
                        aux[0], aux[1], aux[2])

            def score(h):
                q, k, _, bank, _, _ = head_operands(h)
                if h >= 2:
                    pe.wait_ge(scored, 2 * (h - 1) if h < N_HEADS else 2 * h)
                more = h >= N_HEADS
                last = mm(bank[:, 0:128], q[:, 0:P], k[:, 0:P], start=True, stop=not more)
                if more:
                    c0 = ROWS * (h - N_HEADS)
                    mm(bank[:, 0:128], cum[0:1, c0:c0 + P], ones[0:1, 0:P], start=False, stop=False)
                    mm(bank[:, 0:128], ones[0:1, 0:P], ncum[0:1, c0:c0 + P], start=False, stop=True)
                last = mm(bank[:, 128:384], q[:, P:ROWS], k, start=True, stop=not more)
                if more:
                    for half in range(2):
                        mm(bank[:, 128 + P * half:256 + P * half], cum[0:1, c0 + P:c0 + ROWS], ones[0:1, 0:P], start=False, stop=False)
                    last = mm(bank[:, 128:384], ones[0:1, 0:P], ncum[0:1, c0:c0 + ROWS], start=False, stop=True)
                last.then_inc(scores, 1)

            def transpose_probs(h):
                b = h % 2 if h < N_HEADS else 1
                bank = head_operands(h)[4]
                pe.wait_ge(p_scaled, h + 1)
                if h >= 2:
                    pe.wait_ge(pt_copied, h - 1 if h < N_HEADS else h)
                transpose(bank[:, 0:128], probs[:, b, 0:128])
                transpose(bank[:, 128:256], probs[:, b, 129:257])
                transpose(bank[:, 256:384], probs[:, b, 257:385]).then_inc(pt_psum, 1)

            def weigh(h):
                b = h % 2 if h < N_HEADS else 1
                _, _, v, _, _, bank = head_operands(h)
                o = HD * (h % 2)
                pe.wait_ge(pt_copied, h + 1)
                if h < N_HEADS and h >= 4:
                    pe.wait_ge(mix_ready, h // 2 - 1)
                if h >= N_HEADS:
                    pe.wait_ge(sb_ready, 2)
                    if h >= N_HEADS + 2:
                        pe.wait_ge(fox_ready, 1)
                mm(bank[o:o + HD, 0:ROWS], v[:, 0, :], probsT[:, b, 0:ROWS], start=True, stop=False)
                mm(bank[o:o + HD, P:ROWS], v[:, 1, :], probsT[:, b, ROWS:384], start=False, stop=True).then_inc(pv_done, 1)

            pe.wait_ge(acc_free, F_PROJ1)
            pe.wait_ge(tmpT_done, KT * (X_PROJ1 + 1))
            for i in range(N_HEADS + 2):
                if i < N_HEADS:
                    score(i)
                    ada_unit(ADA_FIRST + 2 * i)
                    ada_unit(ADA_FIRST + 2 * i + 1)
                if 1 <= i <= N_HEADS:
                    transpose_probs(i - 1)
                if i >= 2:
                    weigh(i - 2)
                if i >= 2 and i % 2 == 0:
                    if 4 + (i - 2) // 2 < 12:
                        mod_columns(4 + (i - 2) // 2)
            pe.wait_ge(mod_ready, 2)
            pe.wait_ge(mix_ready, 8)
            for k in range(KT):
                wide_unit(U_OUT1 + k, xT[:, k, :], k == 0, k == KT - 1)
                if k == 3:
                    pe.wait_ge(pt_copied, N_HEADS)
                    for g in range(2):
                        pe.wait_ge(g_diag, g + 1)
                        for t in range(KT):
                            ins = mm(aux[2 * g + t // 4][:, P * (t % 4):P * (t % 4 + 1)], ones[:, :], xr[:, g, P * t:P * (t + 1)],
                                     start=True, stop=True)
                        ins.then_inc(g_psum, 1)
            pe.wait_ge(g_ready, 2)
            to_columns(xr, X_UP1, normed, 2)
            pe.wait_ge(resid, RT)
            with pe.Fori(0, D_FF // P // RING) as i:
                for k in range(RING):
                    pe.wait_ge(acc_free, F_PROJ1 - RING + k + 1 + RING * i)
                    col_unit(U_UP1 + k, U_UP1 + k + 1 + RING * i, acc[k], xT, KT * X_UP1 if k == 0 else None)
            pe.wait_ge(acc_free, F_UP1)
            for g in range(4):
                mm(acc[g][:, :], ones[0:1, 0:P], b2row[0:1, 512 * (g % 2):512 * (g % 2) + 512], start=True, stop=False)
            for k in range(D_FF // P):
                pe.wait_ge(hid_ready, RING + k + 1)
                wide_unit(U_DOWN1 + k, hid[:, k, :], False, k == D_FF // P - 1)
            pe.wait_ge(tmpT_done, KT * (X_UP1 + 1))
            for g in range(4):
                ins = transpose(aux[0][:, P * g:P * (g + 1)], wsp[:, g, :])
            ins.then_inc(ws_psum, 1)
            pe.wait_ge(ws_copied, 1)
            to_columns(xr, X_PROJ2, normed, 4)
            pe.wait_ge(resid, 2 * RT)
            for kt in range(KT):
                pe.wait_ge(xT_ready, KT * X_PROJ2 + kt + 1)
            for k in range(22):
                u = U_PROJ2 + k
                if k < 4:
                    narrow_unit(u, k, acc, xT)
                elif k < 8:
                    if k >= 6:
                        pe.wait_ge(acc_free, F_UP1 + k - 5)
                    col_unit(u, u + 1, acc[(2, 3, 0, 1)[k - 4]], xT)
                elif k < 12:
                    if k == 8:
                        pe.wait_ge(acc_free, F_UP1 + 4)
                    narrow_unit(u, k - 8, acc[2:], xT)
                elif k < 16:
                    if k == 12:
                        pe.wait_ge(acc_free, F_UP1 + 6)
                    narrow_unit(u, k - 12, acc, xT)
                else:
                    pe.wait_ge(acc_free, F_UP1 + (7, 8, 9, 10, 11, 12)[k - 16])
                    col_unit(u, u + 1, acc[(2, 3, 0, 1, 2, 3)[k - 16]], xT)
                if k == 17:
                    pe.wait_ge(wf_split, 2)
                    pe.wait_ge(tmpT_done, KT * (X_PROJ2 + 1))
                    for r in range(RT):
                        for kt in range(KT):
                            o = aux[3][:, 4 * r:4 * r + 4]
                            hi, lo = xT[:, kt, P * r:P * (r + 1)], xT[:, kt, ROWS + P * r:ROWS + P * (r + 1)]
                            mm(o, hi, wfh[:, kt, :], start=(kt == 0), stop=False)
                            mm(o, hi, wfl[:, kt, :], start=False, stop=False)
                            ins = mm(o, lo, wfh[:, kt, :], start=False, stop=(kt == KT - 1))
                    ins.then_inc(f_psum, 1)
            for n in range(N_BRANCH):
                for k in range(KT + 2):
                    i = n * (KT + 2) + k
                    u = U_GB + i
                    if k < KT:
                        if k == 0 and n == 0:
                            pe.wait_ge(acc_free, F_PROJ2)
                            pe.wait_ge(xc_ready, 2)
                        wide_unit(u, xT[:, k, :], k == 0, k == KT - 1, (branch_done, 4 * (n - 1)) if k == 0 and n else None)
                    else:
                        if k == KT:
                            done, count = ((conv_ready, 2), (y_ready, 2), (sb_ready, 2), (fox_ready, 2))[n]
                            pe.wait_ge(done, count)
                        wide_unit(u, yT[:, 2 * n + k - KT, :], k == KT, k == KT + 1, (sig_done, 4 * n) if k == KT else None)
                    for step, h in GB_STEPS.get(i, []):
                        if step == "GMIX":
                            pe.wait_ge(vn_ready, 2)
                            pe.wait_ge(ws_ready, 1)
                            pe.wait_ge(f_added, 1)
                            for g in range(4):
                                ins = mm(aux[3][:, P * g:P * (g + 1)], wspT[:, g, :], vn[:, :, HD * g:HD * (g + 1)], start=True, stop=True)
                            ins.then_inc(gmix_done, 1)
                        elif step == "GT":
                            pe.wait_ge(yb_ready, 1)
                            for t in range(2):
                                for r in range(RT):
                                    ins = transpose(aux[3][:, ROWS * t + P * r:ROWS * t + P * (r + 1)], yb[:, r, P * t:P * (t + 1)])
                            ins.then_inc(yb_psum, 1)
                        elif step == "CUM":
                            pe.wait_ge(logf_ready, 1)
                            for g in range(2):
                                for m in range(2):
                                    o = aux[g][0:1, ROWS * m:ROWS * (m + 1)]
                                    hd = 2 * g + m
                                    mm(o, logf[:, 0, hd:hd + 1], upper[:, P:3 * P], start=True, stop=False)
                                    ins = mm(o, logf[:, 1, hd:hd + 1], upper[:, 0:2 * P], start=False, stop=True)
                                ins.then_inc(cum_psum, 1)
                        elif step == "FTQ" or step == "FTK":
                            s = int(step == "FTK")
                            pe.wait_ge(fx_normed, 4)
                            if s == 0:
                                pe.wait_ge(y_ready, 2)
                            for t in range(2):
                                for r in range(RT):
                                    src = (svq[:, r, 256 + P * t:256 + P * (t + 1)], fkv[:, r, P * t:P * (t + 1)])[s]
                                    ins = transpose(aux[3 - s][:, ROWS * t + P * r:ROWS * t + P * (r + 1)], src)
                            ins.then_inc(fx_psum, 1)
                        elif step == "Z":
                            o = HD * (h % 2)
                            q, kk = sbT[o:o + HD, h // 2, :], sbT[o:o + HD, 2 + h // 2, :]
                            if h == 0:
                                pe.wait_ge(cum_ready, 1)
                            else:
                                pe.wait_ge(sp_made, h)
                            mm(aux[0][:, 0:ROWS], kk[:, 0:P], q, start=True, stop=True)
                            mm(aux[0][:, ROWS:384], kk[:, P:], q[:, P:], start=True, stop=True).then_inc(z_psum, 1)
                        elif step == "ARG":
                            o = HD * (h % 2)
                            q, kk = sbT[o:o + HD, h // 2, :], sbT[o:o + HD, 2 + h // 2, :]
                            pe.wait_ge(sp_masked, h + 1)
                            if h >= 1:
                                pe.wait_ge(w_exped, h)
                            bank, spl = aux[1], probs[:, 0, 0:384]
                            mm(bank[:, 0:ROWS], kk[:, 0:P], q, start=True, stop=False)
                            mm(bank[:, 0:ROWS], neg_ge[:, :], spl[:, 0:ROWS], start=False, stop=False)
                            mm(bank[:, P:ROWS], neg_ones[:, :], spl[:, ROWS:384], start=False, stop=True)
                            mm(bank[:, ROWS:384], kk[:, P:], q[:, P:], start=True, stop=False)
                            mm(bank[:, ROWS:384], neg_ge[:, :], spl[:, ROWS:384], start=False, stop=True).then_inc(arg_psum, 1)
                        elif step == "PVS":
                            o = HD * (h % 2)
                            pe.wait_ge(w_masked, h + 1)
                            if h == 0:
                                pe.wait_ge(fxT_ready, 2)
                            if h == 2:
                                pe.wait_ge(sb_ready, 1)
                            mm(aux[2][o:o + HD, 0:ROWS], svq[:, 0, HD * h:HD * (h + 1)], probsT[:, 0, 0:ROWS], start=True, stop=False)
                            mm(aux[2][o:o + HD, P:ROWS], svq[:, 1, HD * h:HD * (h + 1)], probsT[:, 0, ROWS:384],
                               start=False, stop=True).then_inc(pvs_done, 1)
                        elif step == "QK":
                            score(h)
                        elif step == "TR":
                            transpose_probs(h)
                        elif step == "PV":
                            weigh(h)
            pe.wait_ge(fox_ready, 2)
            to_columns(merged, X_OUT2, branch_done, 4 * N_BRANCH - RT)
            for k in range(KT):
                pe.wait_ge(xT_ready, KT * X_OUT2 + k + 1)
                wide_unit(U_OUT2 + k, xT[:, k, :], k == 0, k == KT - 1)
            to_columns(xr, X_UP2, normed, 6)
            pe.wait_ge(resid, 3 * RT)
            with pe.Fori(0, FF2 // P // 2) as i:
                for k in range(RING):
                    pe.wait_ge(acc_free, F_PROJ2 - 2 + 2 * (k // 2) + RING * i)
                    col_unit(U_UP2 + k, U_UP2 + k + 1 + RING * i, acc[k], xT, KT * X_UP2 if k == 0 else None)
            for k in range(FF2 // P):
                if k == 0:
                    pe.wait_ge(acc_free, F_PROJ2 + 2 * FF2 // P)
                pe.wait_ge(hid_ready, RING + D_FF // P + k + 1)
                wide_unit(U_DOWN2 + k, hid[:, k, :], k == 0, k == FF2 // P - 1)


def bucket_table():
    dist = 255 - np.arange(DIST)
    n = np.maximum(dist, 0)
    exact = N_BUCKETS // 2
    large = exact + (np.log(np.maximum(n, 1).astype(np.float32) / exact) / np.float32(np.log(MAX_DISTANCE / exact))
                     * (N_BUCKETS - exact)).astype(np.int32)
    bucket = np.where(n < exact, n, np.minimum(large, N_BUCKETS - 1))
    t = np.zeros((WMASK_ROW + 1, DIST), np.float32)
    t[bucket, np.arange(DIST)] = 1.0
    t[N_BUCKETS, dist < 0] = NEG
    t[WMASK_ROW, dist >= WINDOW] = NEG
    return t


_INS = ["x", "c", "w_in", "w_out", "sinks", "rel_bias", "w_ada", "b_ada", "norm_gains", "w1", "b1", "w2", "b2",
        "norm_mix_g_2", "w_in_2", "w_conv_2", "w_spatial_2", "b_spatial_2", "gmlp_ln_g_2", "gmlp_ln_b_2",
        "fox_q_norm_g_2", "fox_k_norm_g_2", "fox_forget_b_2", "w_branch_2", "w_out_2", "norm_ffn_g_2",
        "w_ffn_in_2", "w_ffn_out_2"]


def kernel(**inputs):
    import concourse.bacc as bacc
    from concourse.bass_utils import run_bass_kernel_spmd

    nc = bacc.Bacc("TRN2", target_bir_lowering=False, num_devices=1)
    arrays, aps = {}, {}
    for name in _INS:
        arr = np.ascontiguousarray(inputs[name])
        arrays["in_" + name] = arr
        aps[name] = nc.dram_tensor("in_" + name, arr.shape, mybir.dt.from_np(arr.dtype), kind="ExternalInput").ap()
    table = bucket_table()
    arrays["bucket_onehot"] = table
    aps["bucket_onehot"] = nc.dram_tensor("bucket_onehot", table.shape, mybir.dt.float32, kind="ExternalInput").ap()
    aps["out"] = nc.dram_tensor("out_rows", (1, ROWS, D), mybir.dt.float32, kind="ExternalOutput").ap()
    build_program(nc, aps)
    r = run_bass_kernel_spmd(nc, [arrays], core_ids=[0])
    return r.results[0]["out_rows"]
```

```python
import numpy as np

import concourse.bass as bass
from concourse import mybir
from contextlib import ExitStack

P = 128
ROWS = 256
RT = ROWS // P
D = 1024
KT = D // P
HD = 64
SCALE = HD ** -0.5
EPS = 1e-6
NEG = -1e30
BIG = 3e38
N_HEADS = 16
N_MOBA = 8
N_KV = 2
WINDOW = 128
N_BUCKETS = 32
MAX_DISTANCE = 128
W_A = N_MOBA * HD
W_KV = N_KV * HD
D_IN = 3 * W_A + (N_HEADS - N_MOBA) * HD + 2 * W_KV
D_FF = 4 * D
MIX = 256
FF2 = 2816
N_BRANCH = 4
UNIT = 1024
RING = 4
FIRST_RING = 6
AHEAD = 3
DIST = 384
WMASK_ROW = 64
COPIES = 16
AUG = 36

C_CB, C_CC, C_CX, C_UV = 0, MIX, 2 * MIX, 3 * MIX
C_SBQ, C_SBK, C_SBV = 5 * MIX, 6 * MIX, 7 * MIX
C_FXQ, C_FXK, C_FXV, C_F = 8 * MIX, 9 * MIX, 10 * MIX, 11 * MIX
C_GATE = C_F + 4

V_N0, V_N2, V_C, V_EARLY = 0, 8, 16, 24
V_B1, V_NMIX, V_NFFN, V_CONV, V_GQ, V_GK, V_BSP, V_ROWS = 24, 56, 64, 72, 78, 79, 80, 84
C_SH1, C_SC1, C_G1, C_SH2, C_SC2, C_G2 = range(6)
M_SH1, M_SC1, M_SH2, M_SC2 = 0, 8, 16, 24

U_PROJ1 = 0
U_OUT1 = U_PROJ1 + D_IN // P
U_UP1 = U_OUT1 + KT
U_DOWN1 = U_UP1 + D_FF // P
U_PROJ2 = U_DOWN1 + D_FF // P
U_GB = U_PROJ2 + 22
U_OUT2 = U_GB + N_BRANCH * (KT + 2)
U_UP2 = U_OUT2 + KT
U_DOWN2 = U_UP2 + 2 * FF2 // P
U_END = U_DOWN2 + FF2 // P
ADA_FIRST = 2 * KT
ADA_UNITS = 5 * KT


def ada_after(u):
    return {5: 1, 6: 1, 7: 1, 8: 1, 9: 1, 10: 1, 11: 1, 12: 1, 13: 1, 14: 1, 15: 1, 16: 1, 17: 2, 18: 2, 19: 2, 20: 3, 21: 3}.get(u, 0)


def ada_units_after(u):
    first = ADA_FIRST + sum(ada_after(v) for v in range(u))
    return list(range(first, first + ada_after(u)))


def first_stream():
    order = [("ada", i) for i in range(ADA_FIRST)]
    i = ADA_FIRST
    for u in range(U_UP1):
        order.append(("w", u))
        order += [("ada", i + j) for j in range(ada_after(u))]
        i += ada_after(u)
    assert i == ADA_UNITS
    return order


BIAS_AFTER = [5, 17]

STREAM = first_stream()
PLACE = {item: place for place, item in enumerate(STREAM)}


def raw_place(u):
    if u < U_UP1:
        place = PLACE[("w", u)]
        return place % FIRST_RING, place // FIRST_RING + 1
    return u % RING, (u - U_UP1) // RING + 1


PROJ_SLOTS = {0: [12, 13], 1: [14], 2: [15, 16], 3: [17]}
OUT_SLOT = 5
SPLIT_SLOTS = {0: [15, 16], 1: [17], 2: [18], 4: [19], 6: [20], 8: [21], 10: [22], 12: [23], 14: [24], 16: [25], 17: [26]}

ROWS_OUT1, ROWS_DOWN1, ROWS_GATE0, ROWS_OUT2, ROWS_DOWN2 = 0, 1, 2, 10, 11

F_PROJ1 = 15
F_UP1 = F_PROJ1 + D_FF // P
F_PROJ2 = F_UP1 + 14

N_IN1, N_Y1, N_FF1, N_Y2, N_MIX, N_FF2 = range(6)
RSTD_ORDER = [(N_IN1, 0), (N_IN1, 1), (N_Y1, 0), (N_FF1, 0), (N_Y1, 1), (N_FF1, 1),
              (N_Y2, 0), (N_MIX, 0), (N_Y2, 1), (N_MIX, 1), (N_FF2, 0), (N_FF2, 1)]
SQUARE_ORDER = [(n, r) for n in (N_IN1, N_FF1, N_MIX, N_FF2) for r in range(RT)]
X_PROJ1, X_UP1, X_PROJ2, X_OUT2, X_UP2 = range(5)
X_COUNT = RT * KT

PE_STEPS = {
    ("GMIX", 0): 0, ("LOGT", 0): 2, ("GT", 0): 3, ("CUM", 0): 4, ("FTQ", 0): 4, ("FTK", 0): 6, ("Z", 0): 8,
    ("ARG", 0): 12, ("Z", 1): 12, ("PVS", 0): 13, ("ARG", 1): 14, ("Z", 2): 15, ("PVS", 1): 17, ("ARG", 2): 20,
    ("Z", 3): 20, ("PVS", 2): 22, ("QK", 16): 22, ("ARG", 3): 23, ("PVS", 3): 25, ("TR", 16): 25, ("QK", 17): 25,
    ("PV", 16): 27, ("TR", 17): 29, ("QK", 18): 29, ("PV", 17): 31, ("QK", 19): 31, ("TR", 18): 33, ("PV", 18): 34,
    ("TR", 19): 34, ("PV", 19): 36,
}
ACT_STEPS = {
    ("LOGF", 0): 0, ("LOGT", 0): 2, ("CUM", 0): 4, ("FTQ", 0): 6, ("FTK", 0): 8, ("Z", 0): 9, ("ARG", 0): 12,
    ("Z", 1): 13, ("ARG", 1): 14, ("Z", 2): 15, ("ARG", 2): 20, ("Z", 3): 21, ("QK", 16): 23, ("ARG", 3): 24,
    ("TR", 16): 25, ("QK", 17): 25, ("TR", 17): 29, ("QK", 18): 31, ("TR", 18): 32, ("QK", 19): 32, ("TR", 19): 36,
}
DVE_STEPS = {
    ("GMIX", 0): 0, ("LOGF", 0): 0, ("GT", 0): 2, ("Z", 0): 10, ("ARG", 0): 12, ("Z", 1): 13, ("ARG", 1): 14,
    ("Z", 2): 16, ("ARG", 2): 20, ("PVS", 1): 21, ("Z", 3): 21, ("QK", 16): 22, ("SCALE", 16): 23, ("ARG", 3): 24,
    ("PVS", 3): 25, ("QK", 17): 25, ("SCALE", 17): 26, ("QK", 18): 29, ("PV", 17): 30, ("SCALE", 18): 30,
    ("QK", 19): 31, ("SCALE", 19): 32, ("PV", 19): 36,
}


def steps_at(table, i):
    return [item for item, unit in table.items() if unit == i]


def build_program(nc, a):
    f32, f32r = mybir.dt.float32, mybir.dt.float32r
    ACT = mybir.ActivationFunctionType
    ALU = mybir.AluOpType
    AX = mybir.AxisListType

    w_in = a["w_in"][0].rearrange("(t p) n -> p t n", p=P)
    w_out = a["w_out"][0]
    w1 = a["w1"][0].rearrange("(t p) n -> p t n", p=P)
    w2 = a["w2"][0]
    w_ada = a["w_ada"][0].rearrange("(t p) n -> p t n", p=P)
    w_ada_rows = a["w_ada"][0]
    w_in2 = a["w_in_2"][0].rearrange("(t p) n -> p t n", p=P)
    w_in2_rows = a["w_in_2"][0]
    w_branch = a["w_branch_2"][0]
    w_out2 = a["w_out_2"][0]
    w_up2 = a["w_ffn_in_2"][0].rearrange("(t p) n -> p t n", p=P)
    w_down2 = a["w_ffn_out_2"][0]
    norm_gains = a["norm_gains"][0]
    x_dram = a["x"][0].rearrange("(r p) n -> p r n", p=P)
    out_dram = a["out"][0].rearrange("(r p) n -> p r n", p=P)
    bias_dram = nc.dram_tensor("bias_by_distance", [N_HEADS, COPIES, DIST], f32, kind="Internal").ap()

    ctx = ExitStack()
    with ctx:
        def sb(name, shape, dt=f32, scope=ctx):
            return scope.enter_context(nc.sbuf_tensor(name, shape, dt))

        def sem(name):
            return ctx.enter_context(nc.semaphore(name))

        raw = sb("raw", [P, RING, UNIT])
        wh = sb("wh", [P, RING, UNIT], f32r)
        wl = sb("wl", [P, RING, UNIT], f32r)
        x = sb("x_rows", [P, RT, D])
        xr = sb("rows_tmp", [P, RT, D])
        xT = sb("xT", [P, KT, 2 * ROWS], f32r)
        tmpT = sb("tmpT", [P, 4, ROWS])
        act_t = sb("act_t", [P, 4, ROWS])
        val_t = sb("val_t", [P, 4, ROWS])
        vrows = sb("vrows", [V_EARLY, P])
        vrows2 = sb("vrows2", [V_ROWS - V_EARLY, P])
        vT = sb("vT", [P, V_ROWS])
        cT = sb("cT", [P, KT])
        modT = sb("modT", [P, 4 * KT])
        A1 = sb("A1", [P, KT])
        A2 = sb("A2", [P, KT])
        G1 = sb("G1", [P, D])
        G2 = sb("G2", [P, D])
        b2row = sb("b2row", [1, D])
        ident = sb("ident", [P, P])
        ones = sb("ones", [P, P])
        neg_ge = sb("neg_ge", [P, P])
        neg_ones = sb("neg_ones", [P, P])
        upper = sb("upper", [P, 3 * P])
        causal = sb("causal", [P, ROWS])
        mhalf = sb("mhalf", [P, 16])
        big = sb("big", [P, 1])
        relw = sb("relw", [WMASK_ROW + 1, N_HEADS])
        onehot = sb("onehot", [WMASK_ROW + 1, DIST])
        dist_rows = sb("dist_rows", [N_HEADS, DIST])
        sinks = sb("sinks_b", [P, 8])
        nsink = sb("nsink", [P, 8])
        bf = sb("bf_col", [4, 1])
        lng = sb("lng_b", [P, MIX])
        lnb = sb("lnb_b", [P, MIX])
        wsp = sb("wsp", [P, 4, P])
        wspT = sb("wspT", [P, 4, P])
        wf = sb("wf", [P, KT, 4])
        wfh = sb("wfh", [P, KT, 4], f32r)
        wfl = sb("wfl", [P, KT, 4], f32r)
        ss = sb("ss", [P, 6, RT, 2])
        ms = sb("ms", [P, 6, RT])
        rstd = sb("rstd", [P, 6, RT])
        logits = sb("logits", [P, 2, 386])
        probs = sb("probs", [P, 2, 386])
        probsT = sb("probsT", [P, 2, 384])
        nmax = sb("nmax", [P, 20, RT])
        lsum = sb("lsum", [P, 20, RT])
        rsum = sb("rsum", [P, 20, RT])
        fraw = sb("fraw", [4, ROWS])
        ft = sb("ft", [4, ROWS])
        logfT = sb("logfT", [4, ROWS])
        logf = sb("logf", [P, RT, 4])
        bnst = sb("bnst", [P, RT, 6])
        bnag = sb("bnag", [P, RT, 2])
        ln_ms = sb("ln_ms", [P, RT])
        ln_rstd = sb("ln_rstd", [P, RT])
        fx_ss = sb("fx_ss", [P, RT, 8])
        fx_ms = sb("fx_ms", [P, RT, 8])
        fx_rstd = sb("fx_rstd", [P, RT, 8])
        gqs = sb("gqs", [P, 1])
        with ExitStack() as s1:
            hid = sb("hid", [P, D_FF // P, 2 * ROWS], f32r, s1)
        with ExitStack() as s2:
            qT = sb("qT", [P, 8, ROWS], f32, s2)
            kT = sb("kT", [P, 6, ROWS], f32, s2)
            vall = sb("vall", [P, RT, W_A + W_KV], f32, s2)
            dbias = sb("dbias", [P, N_HEADS, ROWS], f32, s2)
            ada_sum = sb("ada_sum", [P, 5 * D], f32, s2)
            raw_more = sb("raw_more", [P, FIRST_RING - RING, UNIT], f32, s2)
        with ExitStack() as s3:
            yT = sb("yT", [P, 8, 2 * ROWS], f32r, s3)
            sig = sb("sig", [P, RT, D], f32, s3)
            gu = sb("gu", [P, RT, 2 * MIX], f32, s3)
            vn = sb("vn", [P, RT, MIX], f32, s3)
            yb = sb("yb", [P, RT, MIX], f32, s3)
            svq = sb("svq", [P, RT, 512], f32, s3)
            fkv = sb("fkv", [P, RT, 512], f32, s3)
            fsq = sb("fsq", [P, 512], f32, s3)
            z_sb = fsq[:, 0:384]
            sbT = sb("sbT", [P, 4, ROWS], f32, s3)
            cbc = sb("cbc", [P, 4, ROWS], f32, s3)
            xcp = sb("xcp", [P, 2, ROWS + 2], f32, s3)
            fT = sb("fT", [P, 4, ROWS], f32, s3)
            cumq = sb("cumq", [P, 4, ROWS], f32, s3)
            cumk = sb("cumk", [P, 4, ROWS], f32, s3)
        merged = xr

        acc = [ctx.enter_context(nc.psum_tensor(f"acc{i}", [P, 512], f32)) for i in range(4)]
        aux = [ctx.enter_context(nc.psum_tensor(f"aux{i}", [P, 512], f32)) for i in range(4)]

        first_full = [sem(f"first_full{i}") for i in range(FIRST_RING)]
        raw_full = [sem(f"raw_full{i}") for i in range(RING)]
        rounded, split_ready, unit_done, rows_ready = sem("rounded"), sem("split_ready"), sem("unit_done"), sem("rows_ready")
        acc_free = sem("acc_free")
        ada_zeroed, ada_zeroed2, ada_bias, ada_bias2 = (sem(n) for n in ("ada_zeroed", "ada_zeroed2", "ada_bias", "ada_bias2"))
        ada_used, gain_scaled, g2_full, g2_used = (sem(n) for n in ("ada_used", "gain_scaled", "g2_full", "g2_used"))
        mod_psum, mod_summed, mod_ready = sem("mod_psum"), sem("mod_summed"), sem("mod_ready")
        shift_summed = sem("shift_summed")
        vec2_loaded, gain_loaded = sem("vec2_loaded"), sem("gain_loaded")
        gain2_loaded, late_loaded = sem("gain2_loaded"), sem("late_loaded")
        x_loaded, vec_loaded, misc_loaded = sem("x_loaded"), sem("vec_loaded"), sem("misc_loaded")
        bias_loaded = [sem("bias_loaded_moba"), sem("bias_loaded_window")]
        consts_made, relw_zeroed, relw_made = sem("consts_made"), sem("relw_zeroed"), sem("relw_made")
        vec_cols, vec_ready, c_ready = sem("vec_cols"), sem("vec_ready"), sem("c_ready")
        dist_done, dist_copied, dist_stored = sem("dist_done"), sem("dist_copied"), sem("dist_stored")
        bank_squared = sem("bank_squared")
        ss_ready, rstd_ready, normed, resid = sem("ss_ready"), sem("rstd_ready"), sem("normed"), sem("resid")
        nt_ready, tmpT_done, xT_ready = sem("nt_ready"), sem("tmpT_done"), sem("xT_ready")
        sums_inverted = sem("sums_inverted")
        scores, scored, exped, p_scaled = sem("scores"), sem("scored"), sem("exped"), sem("p_scaled")
        pt_psum, pt_copied, pv_done, mix_ready = sem("pt_psum"), sem("pt_copied"), sem("pv_done"), sem("mix_ready")
        nsink_made = sem("nsink_made")
        g_psum, g_ready = sem("g_psum"), sem("g_ready")
        hid_hi, hid_sq, hid_ready, silu_done = sem("hid_hi"), sem("hid_sq"), sem("hid_ready"), sem("silu_done")
        sig_done, merged_ready = sem("sig_done"), sem("merged_ready")
        gated_out = sem("gated_out")
        wf_split, f_psum, f_added, f_abs = (sem(n) for n in ("wf_split", "f_psum", "f_added", "f_abs"))
        f_e, f_l, logf_ready = sem("f_e"), sem("f_l"), sem("logf_ready")
        cum_psum, cum_ready, aug_made = sem("cum_psum"), sem("cum_ready"), sem("aug_made")
        z_copied, arg_made = sem("z_copied"), sem("arg_made")
        logf_psum, logf_copied = sem("logf_psum"), sem("logf_copied")
        ws_psum, ws_copied, ws_ready = sem("ws_psum"), sem("ws_copied"), sem("ws_ready")
        ln_stat, ln_rstd_ready, vn_ready, gmix_done, yb_ready, yb_psum = (sem(n) for n in ("ln_stat", "ln_rstd_ready", "vn_ready", "gmix_done", "yb_ready", "yb_psum"))
        y_ready = sem("y_ready")
        xc_ready, conv_ready = sem("xc_ready"), sem("conv_ready")
        fx_stat, fx_rstd_ready, fx_normed, fx_psum, fxT_ready = (sem(n) for n in ("fx_stat", "fx_rstd_ready", "fx_normed", "fx_psum", "fxT_ready"))
        z_psum, z_abs, z_exp, z_ln, sp_made, sp_masked = (sem(n) for n in ("z_psum", "z_abs", "z_exp", "z_ln", "sp_made", "sp_masked"))
        arg_psum, w_exped, w_masked, pvs_done, sb_ready, fox_ready = (sem(n) for n in ("arg_psum", "w_exped", "w_masked", "pvs_done", "sb_ready", "fox_ready"))
        dve_step, pool_step = sem("dve_step"), sem("pool_step")
        out_ready, out_done = sem("out_ready"), sem("out_done")

        block = ctx.enter_context(nc.Block())

        def slot_of(u):
            return u % RING

        def raw_slot(r):
            return raw[:, r, :] if r < RING else raw_more[:, r - RING, :]

        def col_src(w, col):
            return w[:, :, col:col + P]

        def proj1_col(k):
            if k < 8:
                return k * P
            if 12 <= k < 16:
                return 3 * W_A + (k - 12) * P
            return 3 * W_A + 512 + (k - 16) * P

        PROJ2 = ([("narrow", C_UV, g) for g in range(4)]
                 + [("col", C_SBQ + P * i, 0) for i in range(4)]
                 + [("narrow", C_SBV, g) for g in range(4)]
                 + [("narrow", C_FXK, g) for g in range(4)]
                 + [("col", C_CB + P * i, 0) for i in range(6)])

        @block.sync
        def _(sp):
            def full(k):
                return raw_full[k % RING]

            def slot8(k):
                return raw[:, k % RING, :].rearrange("p (t n) -> p t n", t=KT)

            def slot2(k):
                return raw[:, k % RING, :].rearrange("p (t n) -> p t n", t=2)


            def slot_free(place):
                if place >= FIRST_RING:
                    kind, i = STREAM[place - FIRST_RING]
                    sp.wait_ge(ada_used if kind == "ada" else split_ready, i + 1)

            def free(u):
                sp.wait_ge(split_ready, u - RING + 1)

            for place, (kind, k) in enumerate(STREAM):
                slot_free(place)
                slot, done = raw_slot(place % FIRST_RING), first_full[place % FIRST_RING]
                if kind == "ada":
                    chunk, kt = divmod(k, KT)
                    sp.dma_start(slot, w_ada[:, kt, D * chunk:D * (chunk + 1)]).then_inc(done, 16)
                elif 8 <= k < 12:
                    sp.dma_start(slot.rearrange("p (t n) -> p t n", t=2), w_in[:, 2 * (k - 8):2 * (k - 8) + 2, 2 * W_A:3 * W_A]).then_inc(done, 16)
                elif k < U_OUT1:
                    sp.dma_start(slot.rearrange("p (t n) -> p t n", t=KT), col_src(w_in, proj1_col(k))).then_inc(done, 16)
                else:
                    sp.dma_start(slot, w_out[P * (k - U_OUT1):P * (k - U_OUT1 + 1), :]).then_inc(done, 16)
                if place == 0:
                    sp.wait_ge(ada_zeroed, 2)
                    sp.dma_start(ada_sum[0:1, 0:2 * D], a["b_ada"][:, 0:2 * D]).then_inc(ada_bias, 16)
                if place == 2 * RING - 1:
                    for r in range(RT):
                        sp.dma_start(x[:, r, :], x_dram[:, r, :]).then_inc(x_loaded, 16)
                if kind == "w" and k in BIAS_AFTER:
                    sp.wait_ge(dist_stored, 16)
                    half = BIAS_AFTER.index(k)
                    heads = slice(N_MOBA * half, N_MOBA * (half + 1))
                    for g in range(P // COPIES):
                        sp.dma_start(dbias[COPIES * g:COPIES * (g + 1), heads, :],
                                     bass.AP(tensor=bias_dram.tensor, offset=P - 1 - COPIES * g + N_MOBA * half * COPIES * DIST,
                                             ap=[[DIST - 1, COPIES], [COPIES * DIST, N_MOBA], [1, ROWS]]))\
                            .then_inc(bias_loaded[half], 16)
                if (kind, k) == ("w", U_OUT1):
                    sp.dma_start(G1[:, :], norm_gains[1].partition_broadcast(P)).then_inc(gain_loaded, 16)
                if (kind, k) == ("w", U_UP1 - 1):
                    for dst, src in [
                        (bf[:, :], a["fox_forget_b_2"].rearrange("o h -> h o")),
                        (lng[:, :], a["gmlp_ln_g_2"][0].partition_broadcast(P)),
                        (lnb[:, :], a["gmlp_ln_b_2"][0].partition_broadcast(P)),
                        (b2row[:, :], a["b2"]),
                        (wsp[:, :, :], a["w_spatial_2"][0].rearrange("g t s -> t g s")),
                        (wf[:, :, :], w_in2[:, :, C_F:C_F + 4]),
                    ]:
                        sp.dma_start(dst, src).then_inc(late_loaded, 16)
                    sp.wait_ge(g2_used, 1)
                    sp.dma_start(G2[0:1, :], a["b_ada"][:, D * C_G2:]).then_inc(g2_full, 16)
            sp.wait_ge(ada_used, ADA_UNITS)
            with sp.Fori(0, D_FF // P // RING) as i:
                for k in range(RING):
                    free(U_UP1 + RING * i + k)
                    sp.dma_start(slot8(U_UP1 + k), w1[:, :, bass.ds(RING * P * i + P * k, P)]).then_inc(full(U_UP1 + k), 16)
            sp.dma_start(xr[:, 1, :], norm_gains[3].partition_broadcast(P)).then_inc(gain2_loaded, 16)
            with sp.Fori(0, D_FF // P // RING) as i:
                for k in range(RING):
                    free(U_DOWN1 + RING * i + k)
                    sp.dma_start(raw[:, slot_of(U_DOWN1 + k), :], w2[bass.ds(RING * P * i + P * k, P), :])\
                        .then_inc(full(U_DOWN1 + k), 16)
            for k, (form, col, g) in enumerate(PROJ2):
                free(U_PROJ2 + k)
                if form == "narrow":
                    sp.dma_start(slot2(U_PROJ2 + k), w_in2[:, 2 * g:2 * g + 2, col:col + 512]).then_inc(full(U_PROJ2 + k), 16)
                else:
                    sp.dma_start(slot8(U_PROJ2 + k), col_src(w_in2, col)).then_inc(full(U_PROJ2 + k), 16)
            for n in range(N_BRANCH):
                u0 = U_GB + n * (KT + 2)
                for k in range(KT + 2):
                    free(u0 + k)
                    if k < KT:
                        src = w_in2_rows[P * k:P * (k + 1), C_GATE + D * n:C_GATE + D * (n + 1)]
                    else:
                        src = w_branch[n, P * (k - KT):P * (k - KT + 1), :]
                    sp.dma_start(raw[:, slot_of(u0 + k), :], src).then_inc(full(u0 + k), 16)
            for k in range(KT):
                free(U_OUT2 + k)
                sp.dma_start(raw[:, slot_of(U_OUT2 + k), :], w_out2[P * k:P * (k + 1), :]).then_inc(full(U_OUT2 + k), 16)
            with sp.Fori(0, FF2 // P // 2) as i:
                for k in range(RING):
                    free(U_UP2 + RING * i + k)
                    sp.dma_start(slot8(U_UP2 + k), w_up2[:, :, bass.ds(2 * P * i + FF2 * (k % 2) + P * (k // 2), P)])\
                        .then_inc(full(U_UP2 + k), 16)
            for k in range(FF2 // P):
                free(U_DOWN2 + k)
                sp.dma_start(raw[:, slot_of(U_DOWN2 + k), :], w_down2[P * k:P * (k + 1), :]).then_inc(full(U_DOWN2 + k), 16)
            for g in range(2 * RT):
                sp.wait_ge(out_ready, g + 1)
                cols = slice(512 * (g % 2), 512 * (g % 2) + 512)
                sp.dma_start(out_dram[:, g // 2, cols], x[:, g // 2, cols]).then_inc(out_done, 16)
            sp.wait_ge(out_done, 16 * 2 * RT)

        @block.gpsimd
        def _(pool):
            steps = [0]

            def link(ins):
                steps[0] += 1
                ins.then_inc(pool_step, 1)
                pool.wait_ge(pool_step, steps[0])

            def rsqrt(out, tmp, in_, scale, n, done):
                link(nc.gpsimd.tensor_scalar(tmp, in_, scale, EPS, ALU.mult, ALU.add))
                nc.gpsimd.tensor_tensor(out, tmp, mhalf[:, 0:n], ALU.pow).then_inc(done, 1)

            nc.gpsimd.memset(ada_sum[:, D * C_SC1:D * (C_SC1 + 1)], 0.0).then_inc(ada_zeroed, 1)
            link(nc.gpsimd.memset(ident[:, :], 0.0))
            nc.gpsimd.affine_select(out=ident[:, :], in_=ident[:, :], compare_op=ALU.not_equal, fill=1.0, base=0,
                                    pattern=[[-1, P]], channel_multiplier=1).then_inc(consts_made, 1)
            nc.gpsimd.memset(relw[:, :], 0.0).then_inc(relw_zeroed, 1)
            pool.wait_ge(relw_zeroed, 1)
            nc.gpsimd.memset(relw[N_BUCKETS:N_BUCKETS + 1, :], 1.0).then_inc(relw_made, 1)
            pool.wait_ge(relw_made, 1)
            nc.gpsimd.memset(relw[WMASK_ROW:WMASK_ROW + 1, N_MOBA:], 1.0).then_inc(relw_made, 1)
            pool.wait_ge(relw_made, 2)
            nc.gpsimd.memset(ones[:, :], 1.0)
            nc.gpsimd.memset(neg_ones[:, :], -1.0)
            nc.gpsimd.memset(neg_ge[:, :], -1.0)
            nc.gpsimd.memset(upper[:, :], 1.0)
            nc.gpsimd.memset(causal[:, :], 0.0)
            nc.gpsimd.memset(big[:, :], BIG)
            link(nc.gpsimd.memset(mhalf[:, :], -0.5))
            nc.gpsimd.affine_select(out=neg_ge[:, :], in_=neg_ge[:, :], compare_op=ALU.is_ge, fill=0.0, base=0,
                                    pattern=[[-1, P]], channel_multiplier=1).then_inc(consts_made, 1)
            nc.gpsimd.affine_select(out=upper[:, :], in_=upper[:, :], compare_op=ALU.is_ge, fill=0.0, base=-P,
                                    pattern=[[1, 3 * P]], channel_multiplier=-1).then_inc(consts_made, 1)
            nc.gpsimd.affine_select(out=causal[:, :], in_=causal[:, :], compare_op=ALU.is_ge, fill=NEG, base=P,
                                    pattern=[[-1, ROWS]], channel_multiplier=1).then_inc(consts_made, 1)

            nc.gpsimd.memset(G2[:, :], 0.0).then_inc(g2_used, 1)
            for chunk in range(2, 5):
                nc.gpsimd.memset(ada_sum[:, D * chunk:D * (chunk + 1)], 0.0).then_inc(ada_zeroed2, 1)

            def norm_rstd(n, r):
                if n in (N_Y1, N_Y2):
                    pool.wait_ge(bank_squared, 4 * (N_Y1, N_Y2).index(n) + 2 * r + 2)
                    link(nc.gpsimd.tensor_tensor(ss[:, n, r, 0:1], ss[:, n, r, 0:1], ss[:, n, r, 1:2], ALU.add))
                else:
                    pool.wait_ge(ss_ready, SQUARE_ORDER.index((n, r)) + 1)
                rsqrt(rstd[:, n, r:r + 1], ms[:, n, r:r + 1], ss[:, n, r, 0:1], 1.0 / D, 1, rstd_ready)

            for r in range(RT):
                norm_rstd(N_IN1, r)
            pool.wait_ge(ada_used, (C_G1 + 1) * KT)
            pool.wait_ge(gain_loaded, 16)
            sums = ada_sum[:, D * C_G1:D * (C_G1 + 1)]
            nc.gpsimd.tensor_tensor(sums, sums, G1[:, :], ALU.mult).then_inc(gain_scaled, 1)
            for r in range(RT):
                norm_rstd(N_Y1, r)
                norm_rstd(N_FF1, r)
            pool.wait_ge(g2_used, KT + 1)
            pool.wait_ge(gain2_loaded, 16)
            nc.gpsimd.tensor_tensor(G2[:, :], G2[:, :], xr[:, 1, :], ALU.mult).then_inc(gain_scaled, 1)
            pool.wait_ge(ws_copied, 1)
            nc.gpsimd.affine_select(out=wspT[:, :, :], in_=wspT[:, :, :], compare_op=ALU.is_ge, fill=0.0, base=0,
                                    pattern=[[0, 4], [1, P]], channel_multiplier=-1).then_inc(ws_ready, 1)
            for r in range(RT):
                norm_rstd(N_Y2, r)
                norm_rstd(N_MIX, r)
            nc.gpsimd.memset(cumq[:, :, :], 0.0)
            link(nc.gpsimd.memset(cumk[:, :, :], 0.0))
            for i, (dst, row) in enumerate([(cumk, 0), (cumq, 32), (cumk, 64), (cumq, 96)]):
                onehot_rows = ident[row:row + 4, row:row + 4].unsqueeze(2).to_broadcast([4, 4, ROWS])
                nc.gpsimd.tensor_copy(dst[row:row + 4, :, :], onehot_rows).then_inc(aug_made, 1)
                pool.wait_ge(aug_made, i + 1)
            for r in range(RT):
                pool.wait_ge(ln_stat, r + 1)
                rsqrt(ln_rstd[:, r:r + 1], ln_ms[:, r:r + 1], bnag[:, r, 1:2], 1.0, 1, ln_rstd_ready)
            for r in range(RT):
                pool.wait_ge(fx_stat, 2 * (r + 1))
                rsqrt(fx_rstd[:, r, :], fx_ms[:, r, :], fx_ss[:, r, :], 1.0 / HD, 8, fx_rstd_ready)
            for h in range(4):
                pool.wait_ge(sp_made, h + 1)
                diag = probs[:, 0, 0:384].rearrange("p (b q) -> p b q", b=3)[:, 0:3:2, :]
                nc.gpsimd.affine_select(out=diag, in_=diag, compare_op=ALU.is_gt, fill=0.0, base=0,
                                        pattern=[[0, 2], [1, P]], channel_multiplier=-1).then_inc(sp_masked, 1)
                pool.wait_ge(w_exped, h + 1)
                diag = probsT[:, 0, :].rearrange("p (b q) -> p b q", b=3)[:, 0:3:2, :]
                nc.gpsimd.affine_select(out=diag, in_=diag, compare_op=ALU.is_gt, fill=0.0, base=0,
                                        pattern=[[0, 2], [1, P]], channel_multiplier=-1).then_inc(w_masked, 1)
            for r in range(RT):
                norm_rstd(N_FF2, r)

        @block.scalar
        def _(act):
            A = nc.scalar.activation

            def round_unit(full, raw_unit, wait_full, wait_free, s):
                act.wait_ge(full, wait_full)
                if wait_free is not None:
                    act.wait_ge(unit_done, wait_free)
                A(wh[:, s, :], raw_unit, ACT.Copy).then_inc(rounded, 1)

            def round_static(u):
                if u < U_END:
                    r, count = raw_place(u)
                    full = (first_full if u < U_UP1 else raw_full)[r]
                    round_unit(full, raw_slot(r), 16 * count, u - RING + 1 if u >= RING else None, slot_of(u))

            def round_looped(u0, i, k):
                s, count = raw_place(u0 + k)
                round_unit(raw_full[s], raw_slot(s), 16 * count + 16 * i, u0 + k - RING + 1 + RING * i, s)

            junk = [t[:, :, :].rearrange("p a b -> p (a b)") for t in (act_t, val_t)]

            def square_rows(n, r):
                A(junk[r if n == N_IN1 else 1], x[:, r, :], ACT.Square, accum_out=ss[:, n, r, 0:1]).then_inc(ss_ready, 1)

            def square_banks(n, r, rows, u_last):
                for c in range(2):
                    g = 2 * r + c
                    if g < 3:
                        act.wait_ge(rows_ready, 3 * rows + g + 1)
                    else:
                        act.wait_ge(unit_done, u_last + 1)
                    A(junk[0][:, 512 * c:512 * (c + 1)], acc[g][:, :], ACT.Square, accum_out=ss[:, n, r, c:c + 1])\
                        .then_inc(bank_squared, 1)

            def from_transposed(t, r, kts, scale, bias=None):
                for kt in kts:
                    if kt % 4 == 0:
                        act.wait_ge(nt_ready, 4 * t + 2 * r + kt // 4 + 1)
                    if kt >= 4:
                        act.wait_ge(xT_ready, X_COUNT * t + (4 if r == 0 else KT + 2 * ((kt - 4) // 2 + 1)))
                    elif t > 0:
                        act.wait_ge(xT_ready, X_COUNT * t)
                    src = aux[2 * r + kt // 4][:, P * (kt % 4):P * (kt % 4 + 1)]
                    kw = {} if bias is None else {"bias": bias[:, kt:kt + 1]}
                    A(tmpT[:, kt % 4, P * r:P * (r + 1)], src, ACT.Identity, scale=scale[:, kt:kt + 1], **kw).then_inc(tmpT_done, 1)

            def from_transposed_plain(t, r):
                for half in range(2):
                    act.wait_ge(nt_ready, 4 * t + 2 * r + half + 1)
                    act.wait_ge(xT_ready, X_COUNT * t + (KT * r + 4 if half else 0))
                    A(tmpT[:, :, P * r:P * (r + 1)], aux[2 * r + half][:, :].rearrange("p (t n) -> p t n", t=4), ACT.Copy)\
                        .then_inc(tmpT_done, 4)

            def from_transposed_both(t, scale, bias, units):
                for kt in range(KT):
                    if kt % 2 == 0:
                        act.wait_ge(nt_ready, 4 * t + kt // 2 + 1)
                    if kt >= 4:
                        act.wait_ge(xT_ready, X_COUNT * t + 4 * ((kt - 4) // 2 + 1))
                    A(tmpT[:, kt % 4, :], aux[kt // 2][:, ROWS * (kt % 2):ROWS * (kt % 2) + ROWS], ACT.Identity,
                      scale=scale[:, kt:kt + 1], bias=bias[:, kt:kt + 1]).then_inc(tmpT_done, 2)
                    if kt in units:
                        round_static(units[kt])

            for dst, src in [(vrows[V_C:V_C + KT, :], a["c"][0].rearrange("(t p) -> t p", p=P)),
                             (vrows[V_N0:V_N0 + KT, :], norm_gains[0].rearrange("(t p) -> t p", p=P)),
                             (vrows[V_N2:V_N2 + KT, :], norm_gains[2].rearrange("(t p) -> t p", p=P))]:
                act.dma_start(dst, src).then_inc(vec_loaded, 16)
            act.wait_ge(vec_ready, 1)
            A(cT[:, :], vT[:, V_C:V_C + KT], ACT.Silu).then_inc(c_ready, 1)
            act.wait_ge(ada_zeroed2, 3)
            act.dma_start(ada_sum[0:1, 2 * D:], a["b_ada"][:, 2 * D:5 * D]).then_inc(ada_bias2, 16)
            act.wait_ge(relw_made, 2)
            for dst, src in [
                (relw[0:N_BUCKETS, :], a["rel_bias"]),
                (onehot[:, :], a["bucket_onehot"]),
                (sinks[:, :], a["sinks"][0].partition_broadcast(P)),
            ]:
                act.dma_start(dst, src).then_inc(misc_loaded, 16)
            late = [(V_B1, 32, a["b1"][0].rearrange("(t p) -> t p", p=P)),
                    (V_NMIX, KT, a["norm_mix_g_2"][0].rearrange("(t p) -> t p", p=P)),
                    (V_NFFN, KT, a["norm_ffn_g_2"][0].rearrange("(t p) -> t p", p=P)),
                    (V_CONV, 6, a["w_conv_2"][0].rearrange("j (t p) -> (j t) p", p=P)),
                    (V_BSP, 4, a["b_spatial_2"][0])]
            for row, n, src in late:
                act.dma_start(vrows2[row - V_EARLY:row - V_EARLY + n, :], src).then_inc(vec2_loaded, 16)
            for row, src in ((V_GQ, a["fox_q_norm_g_2"]), (V_GK, a["fox_k_norm_g_2"])):
                for half in range(2):
                    act.dma_start(vrows2[row - V_EARLY:row - V_EARLY + 1, HD * half:HD * (half + 1)], src).then_inc(vec2_loaded, 16)
            for r in range(RT):
                act.wait_ge(x_loaded, 16 * RT)
                square_rows(N_IN1, r)
            act.wait_ge(dist_done, 1)
            A(dist_rows[:, :], aux[1][0:N_HEADS, 0:DIST], ACT.Copy).then_inc(dist_copied, 1)
            act.wait_ge(dist_copied, 1)
            act.dma_start(bias_dram, dist_rows[:, :].unsqueeze(1).to_broadcast([N_HEADS, COPIES, DIST])).then_inc(dist_stored, 16)
            for r in range(RT):
                act.wait_ge(rstd_ready, r + 1)
                A(xr[:, r, :], x[:, r, :], ACT.Copy, scale=rstd[:, N_IN1, r:r + 1]).then_inc(normed, 1)
            act.wait_ge(vec_cols, 2)
            A(vT[:, V_EARLY:], aux[2][:, 0:V_ROWS - V_EARLY], ACT.Copy).then_inc(vec_ready, 1)
            for kt in range(KT):
                act.wait_ge(mod_psum, kt // 4 + 1)
                A(junk[0][:, P * kt:P * (kt + 1)], acc[kt // 4][:, P * (kt % 4):P * (kt % 4 + 1)], ACT.Identity,
                  accum_out=modT[:, M_SH1 + kt:M_SH1 + kt + 1]).then_inc(shift_summed, 1)
            round_static(0)
            act.wait_ge(shift_summed, KT)
            act.wait_ge(mod_ready, 1)
            from_transposed_both(X_PROJ1, A1, modT[:, M_SH1:M_SH1 + KT], {5: 1, 7: 2})

            def leave_bank(k):
                act.wait_ge(unit_done, k + 1)
                bank = acc[k % 4]
                if k < 4:
                    A(qT[:, k, :], bank[:, 0:ROWS], ACT.Copy, scale=SCALE).then_inc(acc_free, 1)
                elif k < 8:
                    A(kT[:, k - 4, :], bank[:, 0:ROWS], ACT.Copy).then_inc(acc_free, 1)
                elif k == 11:
                    A(vall[:, 0, 0:W_A], acc[0][:, :], ACT.Copy)
                    A(vall[:, 1, 0:W_A], acc[1][:, :], ACT.Copy).then_inc(acc_free, 1)
                elif 12 <= k < 16:
                    A(qT[:, k - 8, :], bank[:, 0:ROWS], ACT.Copy, scale=SCALE).then_inc(acc_free, 1)
                elif k == 16:
                    for kv in range(N_KV):
                        for half in range(2):
                            ins = A(kT[HD * half:HD * (half + 1), 4 + kv, :], bank[HD * kv:HD * (kv + 1), 0:ROWS], ACT.Copy)
                    ins.then_inc(acc_free, 1)
                elif k == 17:
                    A(vall[:, :, W_A:], bank[:, 0:ROWS].rearrange("p (r n) -> p r n", r=RT), ACT.Copy).then_inc(acc_free, 1)

            def exp_head(h):
                for r in range(RT):
                    act.wait_ge(scored, 2 * h + r + 1)
                    lo, n = (0, 128) if r == 0 else (129, 256)
                    if N_MOBA <= h < N_HEADS:
                        n += 1
                    if r == 0 and h >= 2:
                        act.wait_ge(pt_psum, h - 1 if h < N_HEADS else h)
                    b = h % 2 if h < N_HEADS else 1
                    A(probs[:, b, lo:lo + n], logits[:, b, lo:lo + n], ACT.Exp, bias=nmax[:, h, r:r + 1], scale=-1.0,
                      accum_out=lsum[:, h, r:r + 1]).then_inc(exped, 1)

            def scale_head(h):
                b = h % 2
                act.wait_ge(sums_inverted, h + 1)
                A(probs[:, b, 0:128], probs[:, b, 0:128], ACT.Copy, scale=rsum[:, h, 0:1])
                A(probs[:, b, 129:385], probs[:, b, 129:385], ACT.Copy, scale=rsum[:, h, 1:2]).then_inc(p_scaled, 1)

            def copy_probsT(h):
                b = h % 2 if h < N_HEADS else 1
                act.wait_ge(pt_psum, h + 1)
                if h >= 2:
                    act.wait_ge(pv_done, h - 1 if h < N_HEADS else h)
                src = aux[2] if h < N_HEADS else aux[1]
                A(probsT[:, b, :], src[:, 0:384], ACT.Copy).then_inc(pt_copied, 1)

            for k in range(11):
                round_static(k + AHEAD)
                leave_bank(k)
            leave_bank(11)
            round_static(11 + AHEAD)
            for i in range(N_HEADS + 2):
                for k in SPLIT_SLOTS.get(i, []):
                    round_static(k)
                if i < N_HEADS:
                    exp_head(i)
                if i < N_HEADS:
                    scale_head(i)
                for k in PROJ_SLOTS.get(i, []):
                    leave_bank(k)
                if 1 <= i <= N_HEADS:
                    copy_probsT(i - 1)

            def gain_rows(g):
                for half in range(2):
                    act.wait_ge(g_psum, 2 * g + half + 1)
                    A((G1, G2)[g][:, 512 * half:512 * (half + 1)], aux[half][:, :], ACT.Copy).then_inc(g_ready, 1)

            round_static(U_UP1 + 1)
            gain_rows(0)
            square_banks(N_Y1, 0, ROWS_OUT1, U_UP1 - 1)
            act.wait_ge(resid, 1)
            square_rows(N_FF1, 0)
            square_banks(N_Y1, 1, ROWS_OUT1, U_UP1 - 1)
            sh2 = modT[:, M_SH2:M_SH2 + KT]
            from_transposed(X_UP1, 0, range(4), A2, sh2)
            act.wait_ge(resid, 2)
            square_rows(N_FF1, 1)
            round_static(U_UP1 + 2)
            from_transposed(X_UP1, 0, range(4, KT), A2, sh2)
            from_transposed(X_UP1, 1, range(KT), A2, sh2)
            with act.Fori(0, D_FF // P // RING) as i:
                for k in range(RING):
                    round_looped(U_UP1 + AHEAD, i, k)
                    act.wait_ge(unit_done, U_UP1 + k + 1 + RING * i)
                    act.wait_ge(hid_ready, RING * i + k + 1)
                    A(act_t[:, k, :], acc[k][:, 0:ROWS], ACT.Relu, bias=vT[:, bass.ds(V_B1 + k + RING * i, 1)]).then_inc(acc_free, 1)
                    act.wait_ge(acc_free, F_PROJ1 + k + 1 + RING * i)
                    A(hid[:, RING * i + k, 0:ROWS], act_t[:, k, :], ACT.Square).then_inc(hid_hi, 1)
                    if k == 1:
                        act.wait_ge(g2_used, i + 1)
                        act.dma_start(xr[:, 0, :], w_ada_rows[bass.ds(P * i, P), D * C_G2:]).then_inc(g2_full, 16)
            with act.Fori(0, D_FF // P // RING - 1) as i:
                for k in range(RING):
                    round_looped(U_DOWN1 + AHEAD, i, k)
            round_static(U_PROJ2 - 1)
            gain_rows(1)
            act.wait_ge(ws_psum, 1)
            A(wspT[:, :, :], aux[2][:, :].rearrange("p (g t) -> p g t", g=4), ACT.Copy).then_inc(ws_copied, 1)
            act.wait_ge(late_loaded, 16 * 6)
            A(wfh[:, :, :], wf[:, :, :], ACT.Copy).then_inc(wf_split, 1)
            square_banks(N_Y2, 0, ROWS_DOWN1, U_PROJ2 - 1)
            round_static(U_PROJ2)
            act.wait_ge(resid, 3)
            square_rows(N_MIX, 0)
            round_static(U_PROJ2 + 1)
            square_banks(N_Y2, 1, ROWS_DOWN1, U_PROJ2 - 1)
            round_static(U_PROJ2 + 2)
            nmix = vT[:, V_NMIX:V_NMIX + KT]
            from_transposed(X_PROJ2, 0, range(KT), nmix)
            act.wait_ge(resid, 4)
            square_rows(N_MIX, 1)
            round_static(U_PROJ2 + 3)
            from_transposed(X_PROJ2, 1, range(KT), nmix)
            for k in range(22):
                if k >= 1:
                    round_static(U_PROJ2 + k + AHEAD)
                act.wait_ge(unit_done, U_PROJ2 + k + 1)
                if k == 3:
                    for r in range(RT):
                        A(gu[:, r, :], acc[r][:, :], ACT.Gelu_apprx_tanh).then_inc(acc_free, 1)
                elif 4 <= k < 6:
                    A(sbT[:, k - 4, :], acc[k - 2][:, 0:ROWS], ACT.Copy, scale=SCALE).then_inc(acc_free, 1)
                elif 6 <= k < 8:
                    A(sbT[:, k - 4, :], acc[k - 6][:, 0:ROWS], ACT.Copy).then_inc(acc_free, 1)
                elif k == 11:
                    for r in range(RT):
                        A(svq[:, r, :], acc[2 + r][:, :], ACT.Copy).then_inc(acc_free, 1)
                elif k == 15:
                    for r in range(RT):
                        A(fkv[:, r, :], acc[r][:, :], ACT.Copy).then_inc(acc_free, 1)
                elif 16 <= k < 20:
                    A(cbc[:, k - 16, :], acc[(2, 3, 0, 1)[k - 16]][:, 0:ROWS], ACT.Copy).then_inc(acc_free, 1)
            def softplus_parts(h):
                act.wait_ge(z_psum, h + 1)
                buf = logits[:, 0, 0:384]
                if h >= 1:
                    act.wait_ge(w_exped, h)
                A(buf, aux[0][:, 0:384], ACT.Abs).then_inc(z_abs, 1)
                act.wait_ge(z_abs, h + 1)
                A(buf, buf, ACT.Exp, scale=-1.0).then_inc(z_exp, 1)
                act.wait_ge(z_exp, h + 1)
                A(buf, buf, ACT.Ln, bias=1.0).then_inc(z_ln, 1)

            for n in range(N_BRANCH):
                for k in range(KT + 2):
                    i = n * (KT + 2) + k
                    if k != KT - 1:
                        round_static(U_GB + i + AHEAD)
                    if k == KT - 1:
                        for g in range(4):
                            if g < 3:
                                act.wait_ge(rows_ready, 3 * (ROWS_GATE0 + 2 * n) + g + 1)
                            else:
                                act.wait_ge(unit_done, U_GB + i + 1)
                            if n == 1:
                                act.wait_ge(gated_out, g + 1)
                            elif n >= 2:
                                act.wait_ge(merged_ready, 4 * (n - 2) + g + 1)
                            A(sig[:, g // 2, 512 * (g % 2):512 * (g % 2) + 512], acc[g][:, :], ACT.Sigmoid).then_inc(sig_done, 1)
                        round_static(U_GB + i + AHEAD)
                    for step, h in steps_at(ACT_STEPS, i):
                        if step == "LOGF":
                            act.wait_ge(f_psum, 1)
                            A(fraw[:, :], aux[1][0:4, 0:ROWS], ACT.Identity, bias=bf[:, :]).then_inc(f_added, 1)
                            act.wait_ge(f_added, 1)
                            A(ft[:, :], fraw[:, :], ACT.Abs).then_inc(f_abs, 1)
                            act.wait_ge(f_abs, 1)
                            A(ft[:, :], ft[:, :], ACT.Exp, scale=-1.0).then_inc(f_e, 1)
                            act.wait_ge(f_e, 1)
                            A(ft[:, :], ft[:, :], ACT.Ln, bias=1.0).then_inc(f_l, 1)
                        elif step == "CUM":
                            act.wait_ge(cum_psum, 1)
                            act.wait_ge(aug_made, 4)
                            sums = aux[1][0:4, 0:ROWS].unsqueeze(1).to_broadcast([4, 2, ROWS])
                            A(cumq[0:4, 0:4:2, :], sums, ACT.Copy)
                            A(cumk[32:36, 0:4:2, :], sums, ACT.Copy, scale=-1.0)
                            A(cumq[64:68, 1:4:2, :], sums, ACT.Copy)
                            A(cumk[96:100, 1:4:2, :], sums, ACT.Copy, scale=-1.0).then_inc(cum_ready, 1)
                        elif step == "LOGT":
                            act.wait_ge(logf_psum, 1)
                            A(logf[:, :, :], aux[1][:, ROWS:ROWS + 8].rearrange("p (r h) -> p r h", r=RT), ACT.Copy)\
                                .then_inc(logf_copied, 1)
                        elif step == "FTQ" or step == "FTK":
                            s = int(step == "FTK")
                            act.wait_ge(fx_psum, s + 1)
                            gain = (gqs[:, 0:1], vT[:, V_GK:V_GK + 1])[s]
                            A(fT[:, 2 * s:2 * s + 2, :], aux[3 - s][:, :].rearrange("p (t n) -> p t n", t=2), ACT.Identity,
                              scale=gain).then_inc(fxT_ready, 1)
                        elif step == "Z":
                            softplus_parts(h)
                        elif step == "ARG":
                            act.wait_ge(arg_made, h + 1)
                            if h >= 1:
                                act.wait_ge(pvs_done, h)
                            A(probsT[:, 0, :], logits[:, 0, 0:384], ACT.Exp).then_inc(w_exped, 1)
                        elif step == "QK":
                            exp_head(h)
                        elif step == "TR":
                            copy_probsT(h)
            from_transposed_plain(X_OUT2, 0)
            round_static(U_OUT2 + AHEAD)
            from_transposed_plain(X_OUT2, 1)
            for k in range(RING, KT):
                round_static(U_OUT2 + k)
            act.wait_ge(resid, 5)
            square_rows(N_FF2, 0)
            for k in range(AHEAD):
                round_static(U_UP2 + k)
            nffn = vT[:, V_NFFN:V_NFFN + KT]
            from_transposed(X_UP2, 0, range(4), nffn)
            act.wait_ge(resid, 6)
            square_rows(N_FF2, 1)
            from_transposed(X_UP2, 0, range(4, KT), nffn)
            from_transposed(X_UP2, 1, range(KT), nffn)
            with act.Fori(0, FF2 // P // 2) as i:
                for k in range(RING):
                    round_looped(U_UP2 + AHEAD, i, k)
                    if k % 2 == 0:
                        act.wait_ge(unit_done, U_UP2 + k + 1 + RING * i)
                        act.wait_ge(hid_ready, RING + D_FF // P + 2 * i + k // 2 - 1)
                        A(act_t[:, k // 2, :], acc[k][:, 0:ROWS], ACT.Silu).then_inc(silu_done, 1)
            for k in range(FF2 // P):
                round_static(U_DOWN2 + k + AHEAD)

        @block.vector
        def _(dve):
            V = nc.vector
            steps = [0]

            def link(ins):
                steps[0] += 1
                ins.then_inc(dve_step, 1)
                dve.wait_ge(dve_step, steps[0])

            def low_unit(wait, r, s):
                dve.wait_ge(rounded, wait)
                V.tensor_tensor(wl[:, s, :], raw_slot(r), wh[:, s, :].bitcast(f32), ALU.subtract).then_inc(split_ready, 1)

            def low_static(u):
                if u < U_END:
                    low_unit(u + 1, raw_place(u)[0], slot_of(u))

            def split(dst, src, done):
                link(V.tensor_copy(dst[:, 0:ROWS], src))
                V.tensor_tensor(dst[:, ROWS:], src, dst[:, 0:ROWS].bitcast(f32), ALU.subtract).then_inc(done, 1)

            def normalise(n, r):
                dve.wait_ge(rstd_ready, RSTD_ORDER.index((n, r)) + 1)
                V.tensor_scalar(xr[:, r, :], x[:, r, :], rstd[:, n, r:r + 1], None, ALU.mult).then_inc(normed, 1)

            def split_columns(t, r, kts, n):
                for kt in kts[::n]:
                    dve.wait_ge(tmpT_done, X_COUNT * t + KT * r + kt + n)
                    src = tmpT[:, kt % 4:kt % 4 + n, P * r:P * (r + 1)]
                    hi, lo = (xT[:, kt:kt + n, o + P * r:o + P * (r + 1)] for o in (0, ROWS))
                    link(V.tensor_copy(hi, src))
                    V.tensor_tensor(lo, src, hi.bitcast(f32), ALU.subtract).then_inc(xT_ready, n)

            def split_both(t, units):
                for kt in range(0, KT, 2):
                    dve.wait_ge(tmpT_done, X_COUNT * t + 2 * kt + 4)
                    src, dst = tmpT[:, kt % 4:kt % 4 + 2, :], xT[:, kt:kt + 2, :]
                    link(V.tensor_copy(dst[:, :, 0:ROWS], src))
                    V.tensor_tensor(dst[:, :, ROWS:], src, dst[:, :, 0:ROWS].bitcast(f32), ALU.subtract).then_inc(xT_ready, 4)
                    if kt + 1 in units:
                        low_static(units[kt + 1])

            def gated(n, r, c, gain):
                dve.wait_ge(bank_squared, 4 * (N_Y1, N_Y2).index(n) + 2 * r + c + 1)
                cols = slice(512 * c, 512 * (c + 1))
                ins = V.tensor_tensor(xr[:, r, cols], acc[2 * r + c][:, :], gain[:, cols], ALU.mult)
                if c == 1:
                    link(ins)

            def gated_residual(n, r):
                dve.wait_ge(rstd_ready, RSTD_ORDER.index((n, r)) + 1)
                V.scalar_tensor_tensor(out=x[:, r, :], in0=xr[:, r, :], scalar=rstd[:, n, r:r + 1], in1=x[:, r, :],
                                       op0=ALU.mult, op1=ALU.add).then_inc(resid, 1)

            def plain_residual(r, rows, u_last, half_done=None):
                for c in range(2):
                    g = 2 * r + c
                    if g < 3:
                        dve.wait_ge(rows_ready, 3 * rows + g + 1)
                    else:
                        dve.wait_ge(unit_done, u_last + 1)
                    xs = x[:, r, 512 * c:512 * (c + 1)]
                    ins = V.tensor_tensor(xs, acc[g][:, :], xs, ALU.add)
                    if half_done is not None:
                        ins.then_inc(half_done, 1)
                    elif c == 1:
                        ins.then_inc(resid, 1)

            V.memset(ada_sum[:, D * C_SH1:D * (C_SH1 + 1)], 0.0).then_inc(ada_zeroed, 1)
            V.memset(val_t[:, :, :], 0.0).then_inc(hid_ready, RING)
            dve.wait_ge(vec_cols, 1)
            V.tensor_copy(vT[:, 0:V_EARLY], aux[0][:, 0:V_EARLY]).then_inc(vec_ready, 1)
            dve.wait_ge(c_ready, 1)
            dve.wait_ge(ada_bias, 16)
            def ada(i):
                chunk, kt = divmod(i, KT)
                place = PLACE[("ada", i)]
                dve.wait_ge(first_full[place % FIRST_RING], 16 * (place // FIRST_RING + 1))
                if i >= 1:
                    dve.wait_ge(ada_used, i)
                sums = ada_sum[:, D * chunk:D * (chunk + 1)]
                V.scalar_tensor_tensor(out=sums, in0=raw_slot(place % FIRST_RING), scalar=cT[:, kt:kt + 1], in1=sums,
                                       op0=ALU.mult, op1=ALU.add).then_inc(ada_used, 1)

            for i in range(ADA_FIRST):
                ada(i)

            def sum_columns(dst, banks, count, halves=(0, 1)):
                for half in halves:
                    dve.wait_ge(mod_psum, count + half + 1)
                    V.reduce_sum(dst[:, 4 * half:4 * half + 4], banks[half][:, :].rearrange("p (t n) -> p t n", t=4),
                                 axis=AX.X).then_inc(mod_summed, 1)

            sum_columns(modT[:, M_SC1:M_SC1 + KT], acc[2:4], 2)
            dve.wait_ge(mod_summed, 2)
            V.scalar_tensor_tensor(out=A1[:, :], in0=modT[:, M_SC1:M_SC1 + KT], scalar=1.0, in1=vT[:, V_N0:V_N0 + KT],
                                   op0=ALU.add, op1=ALU.mult).then_inc(mod_ready, 1)
            low_static(0)
            split_both(X_PROJ1, {5: 1, 7: 2})
            dve.wait_ge(misc_loaded, 16 * 3)
            V.tensor_scalar(nsink[:, :], sinks[:, :], -1.0, None, ALU.mult).then_inc(nsink_made, 1)
            dve.wait_ge(ada_bias2, 16)
            for k in range(12):
                low_static(k + AHEAD)
                for i in ada_units_after(k + AHEAD):
                    ada(i)

            def score_head(h, bias):
                b = h % 2 if h < N_HEADS else 1
                bank = aux[h % 2] if h < N_HEADS else aux[0]
                first = nsink[:, h - N_MOBA:h - N_MOBA + 1] if N_MOBA <= h < N_HEADS else big[:, 0:1]
                if h >= 2:
                    dve.wait_ge(exped, 2 * (h - 1) if h < N_HEADS else 2 * h)
                if N_MOBA <= h < N_HEADS:
                    V.tensor_copy(logits[:, b, 128:386:257], first.to_broadcast([P, 2]))
                dve.wait_ge(scores, h + 1)
                V.tensor_tensor_reduce(out=logits[:, b, 0:128], in0=bank[:, 0:128], in1=bias[:, 128:256], scale=-1.0,
                                       scalar=first, op0=ALU.add, op1=ALU.min, accum_out=nmax[:, h, 0:1]).then_inc(scored, 1)
                V.tensor_tensor_reduce(out=logits[:, b, 129:385], in0=bank[:, 128:384], in1=bias[:, 0:256], scale=-1.0,
                                       scalar=first, op0=ALU.add, op1=ALU.min, accum_out=nmax[:, h, 1:2]).then_inc(scored, 1)

            def scale_head(h):
                dve.wait_ge(exped, 2 * h + 2)
                link(V.reciprocal(rsum[:, h, :], lsum[:, h, :]))
                V.tensor_scalar(probs[:, 1, 0:128], probs[:, 1, 0:128], rsum[:, h, 0:1], None, ALU.mult)
                V.tensor_scalar(probs[:, 1, 129:385], probs[:, 1, 129:385], rsum[:, h, 1:2], None, ALU.mult).then_inc(p_scaled, 1)

            dve.wait_ge(nsink_made, 1)
            dve.wait_ge(consts_made, 4)
            ada_left = []
            for i in range(N_HEADS + 2):
                if i < N_HEADS:
                    if i % N_MOBA == 0:
                        dve.wait_ge(bias_loaded[i // N_MOBA], 16 * P // COPIES)
                    score_head(i, dbias[:, i, :])
                    if ada_left:
                        ada(ada_left.pop(0))
                    dve.wait_ge(exped, 2 * i + 2)
                    V.reciprocal(rsum[:, i, :], lsum[:, i, :]).then_inc(sums_inverted, 1)
                for k in SPLIT_SLOTS.get(i, []):
                    while len(ada_left) > 1:
                        ada(ada_left.pop(0))
                    low_static(k)
                    ada_left += ada_units_after(k)
                if i not in SPLIT_SLOTS and ada_left:
                    ada(ada_left.pop(0))
                if i >= 3 and i % 2 == 1:
                    p = (i - 3) // 2
                    dve.wait_ge(pv_done, 2 * p + 2)
                    if p == 0:
                        dve.wait_ge(unit_done, U_OUT1)
                    split(xT[:, p, :], aux[3][:, 0:ROWS], mix_ready)
            dve.wait_ge(g_ready, 2)
            gated(N_Y1, 0, 0, G1)
            gated(N_Y1, 0, 1, G1)
            sum_columns(modT[:, M_SH2:M_SH2 + KT], aux[2:4], 4, [0])
            gated_residual(N_Y1, 0)
            sum_columns(modT[:, M_SH2:M_SH2 + KT], aux[2:4], 4, [1])
            sum_columns(modT[:, M_SC2:M_SC2 + KT], aux[0:2], 6)
            dve.wait_ge(mod_summed, 6)
            V.scalar_tensor_tensor(out=A2[:, :], in0=modT[:, M_SC2:M_SC2 + KT], scalar=1.0, in1=vT[:, V_N2:V_N2 + KT],
                                   op0=ALU.add, op1=ALU.mult).then_inc(mod_ready, 1)
            normalise(N_FF1, 0)
            gated(N_Y1, 1, 0, G1)
            gated(N_Y1, 1, 1, G1)
            gated_residual(N_Y1, 1)
            split_columns(X_UP1, 0, range(4), 4)
            low_static(U_UP1 + 1)
            normalise(N_FF1, 1)
            split_columns(X_UP1, 0, range(4, KT), 4)
            split_columns(X_UP1, 1, range(KT), 2)
            low_static(U_UP1 + 2)
            with dve.Fori(0, D_FF // P // RING) as i:
                for k in range(RING):
                    low_unit(U_UP1 + AHEAD + k + 1 + RING * i, slot_of(U_UP1 + AHEAD + k), slot_of(U_UP1 + AHEAD + k))
                    dve.wait_ge(acc_free, F_PROJ1 + k + 1 + RING * i)
                    V.tensor_tensor(val_t[:, k, :], act_t[:, k, :], act_t[:, k, :], ALU.mult).then_inc(hid_sq, 1)
                    dve.wait_ge(hid_sq, RING * i + k + 1)
                    dve.wait_ge(hid_hi, RING * i + k + 1)
                    V.tensor_tensor(hid[:, RING * i + k, ROWS:], val_t[:, k, :], hid[:, RING * i + k, 0:ROWS].bitcast(f32),
                                    ALU.subtract).then_inc(hid_ready, 1)
                dve.wait_ge(g2_full, 16 * i + 32)
                dve.wait_ge(g2_used, i + 1)
                V.scalar_tensor_tensor(out=G2[:, :], in0=xr[:, 0, :], scalar=cT[:, bass.ds(i, 1)], in1=G2[:, :],
                                       op0=ALU.mult, op1=ALU.add).then_inc(g2_used, 1)
            with dve.Fori(0, D_FF // P // RING - 1) as i:
                for k in range(RING):
                    low_unit(U_DOWN1 + AHEAD + k + 1 + RING * i, slot_of(U_DOWN1 + AHEAD + k), slot_of(U_DOWN1 + AHEAD + k))
            dve.wait_ge(wf_split, 1)
            V.tensor_tensor(wfl[:, :, :], wf[:, :, :], wfh[:, :, :].bitcast(f32), ALU.subtract).then_inc(wf_split, 1)
            V.tensor_scalar(gqs[:, :], vT[:, V_GQ:V_GQ + 1], SCALE, None, ALU.mult)
            dve.wait_ge(g_ready, 4)
            low_static(U_PROJ2 - 1)
            gated(N_Y2, 0, 0, G2)
            gated(N_Y2, 0, 1, G2)
            gated_residual(N_Y2, 0)
            low_static(U_PROJ2)
            normalise(N_MIX, 0)
            low_static(U_PROJ2 + 1)
            gated(N_Y2, 1, 0, G2)
            gated(N_Y2, 1, 1, G2)
            split_columns(X_PROJ2, 0, range(4), 2)
            gated_residual(N_Y2, 1)
            split_columns(X_PROJ2, 0, range(4, KT), 2)
            low_static(U_PROJ2 + 2)
            low_static(U_PROJ2 + 3)
            normalise(N_MIX, 1)
            split_columns(X_PROJ2, 1, range(KT), 2)
            V.memset(xcp[:, :, 0:2], 0.0)
            for k in range(22):
                if k >= 1:
                    low_static(U_PROJ2 + k + AHEAD)
                if k == 5:
                    for r in range(RT):
                        dve.wait_ge(acc_free, F_UP1 + r + 1)
                        link(V.bn_stats(bnst[:, r, :], gu[:, r, MIX:]))
                        V.bn_aggr(bnag[:, r, :], bnst[:, r, :]).then_inc(ln_stat, 1)
                if k == 7:
                    for r in range(RT):
                        dve.wait_ge(ln_rstd_ready, r + 1)
                        link(V.tensor_scalar(vn[:, r, :], gu[:, r, MIX:], bnag[:, r, 0:1], ln_rstd[:, r:r + 1],
                                             ALU.subtract, ALU.mult))
                        link(V.tensor_tensor(vn[:, r, :], vn[:, r, :], lng[:, :], ALU.mult))
                        V.tensor_tensor(vn[:, r, :], vn[:, r, :], lnb[:, :], ALU.add).then_inc(vn_ready, 1)
                if k == 17:
                    for r in range(RT):
                        dve.wait_ge(acc_free, F_UP1 + 8 + r + 1)
                        for s, src in enumerate((svq[:, r, 256:512], fkv[:, r, 0:256])):
                            link(V.tensor_tensor(fsq[:, 256 * s:256 * (s + 1)], src, src, ALU.mult))
                            V.reduce_sum(fx_ss[:, r, 4 * s:4 * s + 4],
                                         fsq[:, 256 * s:256 * (s + 1)].rearrange("p (h d) -> p h d", h=4), axis=AX.X)\
                                .then_inc(fx_stat, 1)
                if k == 19:
                    for r in range(RT):
                        dve.wait_ge(fx_rstd_ready, r + 1)
                        for s, src in enumerate((svq[:, r, 256:512], fkv[:, r, 0:256])):
                            v = src.rearrange("p (h d) -> p h d", h=4)
                            V.tensor_tensor(v, v, fx_rstd[:, r, 4 * s:4 * s + 4].unsqueeze(2).to_broadcast([P, 4, HD]),
                                            ALU.mult).then_inc(fx_normed, 1)
                if k == 20 or k == 21:
                    t = k - 20
                    dve.wait_ge(unit_done, U_PROJ2 + k + 1)
                    V.tensor_tensor(xcp[:, t, 2:], acc[2 + t][:, 0:ROWS], cbc[:, 2 + t, :], ALU.mult).then_inc(xc_ready, 1)
            dve.wait_ge(xc_ready, 2)
            for t in range(2):
                wc = [vT[:, V_CONV + 2 * j + t:V_CONV + 2 * j + t + 1] for j in range(3)]
                o = val_t[:, t, :]
                link(V.tensor_scalar(o, xcp[:, t, 2:], wc[2], None, ALU.mult))
                link(V.scalar_tensor_tensor(out=o, in0=xcp[:, t, 1:ROWS + 1], scalar=wc[1], in1=o, op0=ALU.mult, op1=ALU.add))
                link(V.scalar_tensor_tensor(out=o, in0=xcp[:, t, 0:ROWS], scalar=wc[0], in1=o, op0=ALU.mult, op1=ALU.add))
                link(V.tensor_tensor(o, o, cbc[:, t, :], ALU.mult))
                split(yT[:, t, :], o, conv_ready)

            def merge(n, r):
                dve.wait_ge(gated_out, 4 * n + 2 * r + 2)
                V.tensor_tensor(merged[:, r, :], merged[:, r, :], sig[:, r, :], ALU.add).then_inc(merged_ready, 2)

            for n in range(N_BRANCH):
                for k in range(KT + 2):
                    i = n * (KT + 2) + k
                    if k < KT + 1:
                        low_static(U_GB + i + AHEAD)
                    else:
                        for r in range(RT):
                            for g in (2 * r, 2 * r + 1):
                                if g < 3:
                                    dve.wait_ge(rows_ready, 3 * (ROWS_GATE0 + 2 * n + 1) + g + 1)
                                else:
                                    dve.wait_ge(unit_done, U_GB + i + 1)
                                half = slice(512 * (g % 2), 512 * (g % 2) + 512)
                                dst = (merged if n == 0 else sig)[:, r, half]
                                V.tensor_tensor(dst, acc[g][:, :], sig[:, r, half], ALU.mult).then_inc(gated_out, 1)
                            if n == N_BRANCH - 1 and r == 0:
                                merge(n, r)
                        if n < N_BRANCH - 1:
                            low_static(U_GB + i + AHEAD)
                        if 1 <= n < N_BRANCH - 1:
                            for r in range(RT):
                                merge(n, r)
                    for step, h in steps_at(DVE_STEPS, i):
                        if step == "GMIX":
                            dve.wait_ge(gmix_done, 1)
                            for g in range(4):
                                cols = slice(HD * g, HD * (g + 1))
                                ins = V.scalar_tensor_tensor(out=yb[:, :, cols],
                                                             in0=aux[3][:, P * g:P * (g + 1)].rearrange("p (r e) -> p r e", r=RT),
                                                             scalar=vT[:, V_BSP + g:V_BSP + g + 1], in1=gu[:, :, cols],
                                                             op0=ALU.add, op1=ALU.mult)
                            ins.then_inc(yb_ready, 1)
                        elif step == "LOGF":
                            dve.wait_ge(f_l, 1)
                            V.scalar_tensor_tensor(out=logfT[:, :], in0=fraw[:, :], scalar=0.0, in1=ft[:, :],
                                                   op0=ALU.min, op1=ALU.subtract).then_inc(logf_ready, 1)
                        elif step == "GT":
                            dve.wait_ge(yb_psum, 1)
                            for t in range(2):
                                split(yT[:, 2 + t, :], aux[3][:, ROWS * t:ROWS * (t + 1)], y_ready)
                        elif step == "Z":
                            dve.wait_ge(z_ln, h + 1)
                            V.scalar_tensor_tensor(out=probs[:, 0, 0:384], in0=aux[0][:, 0:384], scalar=0.0,
                                                   in1=logits[:, 0, 0:384], op0=ALU.max, op1=ALU.add).then_inc(sp_made, 1)
                            if h >= 1:
                                dve.wait_ge(arg_made, h)
                            V.tensor_copy(z_sb[:, :], aux[0][:, 0:384]).then_inc(z_copied, 1)
                        elif step == "ARG":
                            dve.wait_ge(arg_psum, h + 1)
                            dve.wait_ge(z_copied, h + 1)
                            V.tensor_tensor(logits[:, 0, 0:384], aux[1][:, 0:384], z_sb[:, :], ALU.add).then_inc(arg_made, 1)
                        elif step == "PVS":
                            dve.wait_ge(pvs_done, h + 1)
                            split(yT[:, 4 + h // 2, :], aux[2][:, 0:ROWS], sb_ready)
                        elif step == "QK":
                            score_head(h, causal)
                        elif step == "SCALE":
                            scale_head(h)
                        elif step == "PV":
                            dve.wait_ge(pv_done, h + 1)
                            split(yT[:, 6 + (h - N_HEADS) // 2, :], aux[2][:, 0:ROWS], fox_ready)
            split_columns(X_OUT2, 0, range(4), 4)
            low_static(U_OUT2 + AHEAD - 1)
            merge(N_BRANCH - 1, 1)
            low_static(U_OUT2 + AHEAD)
            split_columns(X_OUT2, 0, range(4, KT), 4)
            split_columns(X_OUT2, 1, range(KT), 4)
            for k in range(RING, KT):
                low_static(U_OUT2 + k)
            plain_residual(0, ROWS_OUT2, U_UP2 - 1)
            normalise(N_FF2, 0)
            low_static(U_UP2)
            plain_residual(1, ROWS_OUT2, U_UP2 - 1)
            split_columns(X_UP2, 0, range(4), 4)
            normalise(N_FF2, 1)
            split_columns(X_UP2, 0, range(4, KT), 4)
            split_columns(X_UP2, 1, range(4), 2)
            low_static(U_UP2 + 1)
            split_columns(X_UP2, 1, range(4, KT), 2)
            low_static(U_UP2 + 2)
            with dve.Fori(0, FF2 // P // 2) as i:
                for k in range(RING):
                    low_unit(U_UP2 + AHEAD + k + 1 + RING * i, slot_of(U_UP2 + AHEAD + k), slot_of(U_UP2 + AHEAD + k))
                    if k % 2 == 1:
                        t = 2 * i + k // 2
                        dve.wait_ge(unit_done, U_UP2 + k + 1 + RING * i)
                        dve.wait_ge(silu_done, t + 1)
                        V.tensor_tensor(val_t[:, k // 2, :], acc[k][:, 0:ROWS], act_t[:, k // 2, :], ALU.mult).then_inc(acc_free, 2)
                        dve.wait_ge(acc_free, F_PROJ2 + 2 * t + 2)
                        V.tensor_copy(hid[:, t, 0:ROWS], val_t[:, k // 2, :]).then_inc(hid_sq, 1)
                        dve.wait_ge(hid_sq, D_FF // P + t + 1)
                        V.tensor_tensor(hid[:, t, ROWS:], val_t[:, k // 2, :], hid[:, t, 0:ROWS].bitcast(f32),
                                        ALU.subtract).then_inc(hid_ready, 1)
            for k in range(FF2 // P):
                low_static(U_DOWN2 + k + AHEAD)
            for r in range(RT):
                plain_residual(r, ROWS_DOWN2, U_END - 1, out_ready)

        @block.tensor
        def _(pe):
            mm = nc.tensor.matmul

            def transpose(out, in_, n=P):
                return mm(out, in_, ident[0:n, 0:n], start=True, stop=True, is_transpose=True)

            def col_unit(u, wait, bank, moving, waits=None):
                s = slot_of(u)
                pe.wait_ge(split_ready, wait)
                for kt in range(KT):
                    if waits is not None:
                        pe.wait_ge(xT_ready, waits(kt))
                    w = slice(P * kt, P * (kt + 1))
                    hi, lo = moving[:, kt, 0:ROWS], moving[:, kt, ROWS:]
                    mm(bank[:, 0:ROWS], wh[:, s, w], hi, start=(kt == 0), stop=False)
                    mm(bank[:, 0:ROWS], wh[:, s, w], lo, start=False, stop=False)
                    ins = mm(bank[:, 0:ROWS], wl[:, s, w], hi, start=False, stop=(kt == KT - 1))
                ins.then_inc(unit_done, 1)

            def three(bank, still, r, s, cols, first, last):
                hi, lo = still[:, P * r:P * (r + 1)], still[:, ROWS + P * r:ROWS + P * (r + 1)]
                mm(bank, hi, wh[:, s, cols], start=first, stop=False)
                mm(bank, hi, wl[:, s, cols], start=False, stop=False)
                return mm(bank, lo, wh[:, s, cols], start=False, stop=last)

            def narrow_half(u, g, bank, still, r):
                s = slot_of(u)
                pe.wait_ge(split_ready, u + 1)
                for j in range(2):
                    ins = three(bank[:, :], still[:, 2 * g + j, :], r, s, slice(512 * j, 512 * (j + 1)),
                                g == 0 and j == 0, g == 3 and j == 1)
                return ins

            def narrow_unit(u, g, banks, still):
                narrow_half(u, g, banks[0], still, 0)
                narrow_half(u, g, banks[1], still, 1).then_inc(unit_done, 1)

            def wide_half(u, still, r, first, last, bank_wait=None):
                s = slot_of(u)
                pe.wait_ge(split_ready, u + 1)
                for g in (2 * r, 2 * r + 1):
                    if bank_wait is not None:
                        pe.wait_ge(bank_wait[0], bank_wait[1] + g + 1)
                    ins = three(acc[g][:, :], still, r, s, slice(512 * (g % 2), 512 * (g % 2) + 512), first, last)
                    if last and g < 3:
                        ins.then_inc(rows_ready, 1)
                return ins

            def wide_unit(u, still, first, last, bank_wait=None):
                wide_half(u, still, 0, first, last, bank_wait)
                wide_half(u, still, 1, first, last, bank_wait).then_inc(unit_done, 1)

            def wide_rows(u0, still, ks, r, first, last):
                for k in ks:
                    ins = wide_half(u0 + k, still(k), r, k == first, k == last)
                    if r == RT - 1:
                        ins.then_inc(unit_done, 1)

            def to_columns(src, r, t, wait, count):
                pe.wait_ge(wait, count)
                for kt in range(KT):
                    ins = transpose(aux[2 * r + kt // 4][:, P * (kt % 4):P * (kt % 4 + 1)], src[:, r, P * kt:P * (kt + 1)])
                    if kt % 4 == 3:
                        ins.then_inc(nt_ready, 1)

            def to_columns_both(src, t, wait):
                for r in range(RT):
                    pe.wait_ge(wait, r + 1)
                    for kt in range(KT):
                        ins = transpose(aux[kt // 2][:, ROWS * (kt % 2) + P * r:ROWS * (kt % 2) + P * (r + 1)],
                                        src[:, r, P * kt:P * (kt + 1)])
                        if r == RT - 1 and kt % 2 == 1:
                            ins.then_inc(nt_ready, 1)

            def columns_ready(t):
                return lambda kt: X_COUNT * t + KT + 2 * (kt // 2) + 2

            def transpose_sums(chunk, banks):
                for t in range(KT):
                    lo = D * chunk + P * t
                    ins = transpose(banks[t // 4][:, P * (t % 4):P * (t % 4 + 1)], ada_sum[:, lo:lo + P])
                    if t % 4 == 3:
                        ins.then_inc(mod_psum, 1)

            def sums_to_rows(sums):
                for half in range(2):
                    mm(aux[half][:, :], ones[:, :], sums[:, 512 * half:512 * (half + 1)], start=True, stop=True).then_inc(g_psum, 1)

            pe.wait_ge(consts_made, 1)
            pe.wait_ge(vec_loaded, 16 * 3)
            transpose(aux[0][:, 0:V_EARLY], vrows[:, :], V_EARLY).then_inc(vec_cols, 1)
            pe.wait_ge(misc_loaded, 16 * 3)
            mm(aux[1][0:N_HEADS, 0:DIST], relw[:, :], onehot[:, :], start=True, stop=True).then_inc(dist_done, 1)
            pe.wait_ge(vec2_loaded, 16 * 9)
            transpose(aux[2][:, 0:V_ROWS - V_EARLY], vrows2[:, :], V_ROWS - V_EARLY).then_inc(vec_cols, 1)
            pe.wait_ge(vec_ready, 2)
            pe.wait_ge(dist_copied, 1)
            to_columns_both(xr, X_PROJ1, normed)
            pe.wait_ge(consts_made, 4)
            pe.wait_ge(ada_used, KT)
            transpose_sums(C_SH1, acc[0:2])
            pe.wait_ge(ada_used, 2 * KT)
            transpose_sums(C_SC1, acc[2:4])
            pe.wait_ge(mod_ready, 1)

            def proj1_unit(k):
                if 8 <= k < 12:
                    if k == 8:
                        pe.wait_ge(acc_free, 6)
                    narrow_unit(k, k - 8, acc, xT)
                elif k < 17:
                    if k >= 4:
                        pe.wait_ge(acc_free, k - 3 if k < 8 else (9, 9, 9, 9, 10)[k - 12])
                    col_unit(k, k + 1, acc[k % 4], xT, (lambda kt: X_COUNT * X_PROJ1 + 4 * (kt // 2) + 4) if k == 0 else None)
                else:
                    pe.wait_ge(acc_free, 11)
                    pe.wait_ge(split_ready, k + 1)
                    for r in range(RT):
                        for kt in range(KT):
                            ins = three(acc[k % 4][:, P * r:P * (r + 1)], xT[:, kt, :], r, slot_of(k), slice(P * kt, P * (kt + 1)),
                                        kt == 0, kt == KT - 1)
                    ins.then_inc(unit_done, 1)

            for k in range(12):
                proj1_unit(k)

            def head_operands(h):
                o = HD * (h % 2)
                if h < N_HEADS:
                    k = kT[o:o + HD, h // 2, :] if h < N_MOBA else kT[o:o + HD, 4 + (h - N_MOBA) // 4, :]
                    vc = HD * h if h < N_MOBA else W_A + HD * ((h - N_MOBA) // 4)
                    return qT[o:o + HD, h // 2, :], k, vall[:, :, vc:vc + HD], aux[h % 2], aux[2], aux[3]
                f = h - N_HEADS
                return (fT[o:o + HD, f // 2, :], fT[o:o + HD, 2 + f // 2, :], fkv[:, :, 256 + HD * f:256 + HD * (f + 1)],
                        aux[0], aux[1], aux[2])

            def score(h):
                q, k, _, bank, _, _ = head_operands(h)
                if h >= 2:
                    pe.wait_ge(scored, 2 * (h - 1) if h < N_HEADS else 2 * h)
                more = h >= N_HEADS
                last = mm(bank[:, 0:128], q[:, 0:P], k[:, 0:P], start=True, stop=not more)
                if more:
                    f, o = h - N_HEADS, HD * (h % 2)
                    cq, ck = cumq[o:o + AUG, f, :], cumk[o:o + AUG, f, :]
                    last = mm(bank[:, 0:128], cq[:, 0:P], ck[:, 0:P], start=False, stop=True)
                last = mm(bank[:, 128:384], q[:, P:ROWS], k, start=True, stop=not more)
                if more:
                    last = mm(bank[:, 128:384], cq[:, P:], ck, start=False, stop=True)
                last.then_inc(scores, 1)

            def transpose_probs(h):
                b = h % 2 if h < N_HEADS else 1
                bank = head_operands(h)[4]
                pe.wait_ge(p_scaled, h + 1)
                if h >= 1:
                    pe.wait_ge(pt_copied, h)
                transpose(bank[:, 0:128], probs[:, b, 0:128])
                transpose(bank[:, 128:256], probs[:, b, 129:257])
                transpose(bank[:, 256:384], probs[:, b, 257:385]).then_inc(pt_psum, 1)

            def weigh(h):
                b = h % 2 if h < N_HEADS else 1
                _, _, v, _, _, bank = head_operands(h)
                o = HD * (h % 2)
                pe.wait_ge(pt_copied, h + 1)
                if 2 <= h < N_HEADS:
                    pe.wait_ge(mix_ready, h // 2)
                if h >= N_HEADS:
                    pe.wait_ge(sb_ready, 2)
                    if h >= N_HEADS + 2:
                        pe.wait_ge(fox_ready, 1)
                mm(bank[o:o + HD, 0:ROWS], v[:, 0, :], probsT[:, b, 0:ROWS], start=True, stop=False)
                mm(bank[o:o + HD, P:ROWS], v[:, 1, :], probsT[:, b, ROWS:384], start=False, stop=True).then_inc(pv_done, 1)

            def out1_half(t, r):
                if t == 0 and r == 0:
                    pe.wait_ge(acc_free, F_PROJ1)
                pe.wait_ge(mix_ready, t + 1)
                ins = wide_half(U_OUT1 + t, xT[:, t, :], r, t == 0, t == KT - 1)
                if r == 1:
                    ins.then_inc(unit_done, 1)

            pe.wait_ge(acc_free, 8)
            pe.wait_ge(xT_ready, X_COUNT * (X_PROJ1 + 1))
            for i in range(N_HEADS + 2):
                if i < N_HEADS:
                    if i == N_MOBA:
                        pe.wait_ge(acc_free, F_PROJ1)
                    score(i)
                for k in PROJ_SLOTS.get(i, []):
                    proj1_unit(k)
                if i >= OUT_SLOT:
                    out1_half((i - OUT_SLOT) // 2, (i - OUT_SLOT) % 2)
                if 1 <= i <= N_HEADS:
                    transpose_probs(i - 1)
                if i >= 2:
                    weigh(i - 2)
            pe.wait_ge(gain_scaled, 1)
            pe.wait_ge(scored, 2 * N_HEADS)
            sums_to_rows(ada_sum[:, D * C_G1:D * (C_G1 + 1)])
            out1_half(KT - 1, 0)
            pe.wait_ge(ada_used, ADA_UNITS)
            pe.wait_ge(pt_copied, N_HEADS)
            transpose_sums(C_SH2, aux[2:4])
            out1_half(KT - 2, 1)
            pe.wait_ge(g_ready, 2)
            transpose_sums(C_SC2, aux[0:2])
            out1_half(KT - 1, 1)
            pe.wait_ge(mod_ready, 2)
            for r in range(RT):
                to_columns(xr, r, X_UP1, normed, RT + r + 1)
            pe.wait_ge(resid, RT)
            with pe.Fori(0, D_FF // P // RING) as i:
                for k in range(RING):
                    pe.wait_ge(acc_free, F_PROJ1 - RING + k + 1 + RING * i)
                    col_unit(U_UP1 + k, U_UP1 + k + 1 + RING * i, acc[k], xT, columns_ready(X_UP1) if k == 0 else None)
            n_hid = D_FF // P
            for k in range(n_hid - RING):
                pe.wait_ge(hid_ready, RING + k + 1)
                wide_unit(U_DOWN1 + k, hid[:, k, :], k == 0, False, (acc_free, F_UP1 - RING) if k == 0 else None)
                if k == n_hid // 2:
                    pe.wait_ge(late_loaded, 16 * 6)
                if n_hid // 2 <= k < n_hid // 2 + 4:
                    g = k - n_hid // 2
                    mm(acc[g][:, :], ones[0:1, 0:P], b2row[0:1, 512 * (g % 2):512 * (g % 2) + 512], start=False, stop=False)
            pe.wait_ge(gain_scaled, 2)
            sums_to_rows(G2)
            for g in range(4):
                ins = transpose(aux[2][:, P * g:P * (g + 1)], wsp[:, g, :])
            ins.then_inc(ws_psum, 1)
            pe.wait_ge(hid_ready, RING + n_hid)
            for r in range(RT):
                wide_rows(U_DOWN1, lambda k: hid[:, k, :], range(n_hid - RING, n_hid), r, None, n_hid - 1)
            pe.wait_ge(g_ready, 4)
            pe.wait_ge(ws_copied, 1)
            to_columns(xr, 0, X_PROJ2, normed, 2 * RT + 1)
            pe.wait_ge(resid, RT + 1)
            for r in range(RT):
                for k in range(4):
                    pe.wait_ge(xT_ready, X_COUNT * X_PROJ2 + KT * r + 2 * k + 2)
                    ins = narrow_half(U_PROJ2 + k, k, acc[r], xT, r)
                    if r == 0 and k == 2:
                        to_columns(xr, 1, X_PROJ2, normed, 2 * RT + 2)
                    if r == 1:
                        ins.then_inc(unit_done, 1)
            pe.wait_ge(resid, 2 * RT)
            for k in range(4, 22):
                u = U_PROJ2 + k
                if k < 8:
                    if k >= 6:
                        pe.wait_ge(acc_free, F_UP1 + k - 5)
                    col_unit(u, u + 1, acc[(2, 3, 0, 1)[k - 4]], xT)
                elif k < 12:
                    if k == 8:
                        pe.wait_ge(acc_free, F_UP1 + 4)
                    narrow_unit(u, k - 8, acc[2:], xT)
                elif k < 16:
                    if k == 12:
                        pe.wait_ge(acc_free, F_UP1 + 6)
                    narrow_unit(u, k - 12, acc, xT)
                else:
                    pe.wait_ge(acc_free, F_UP1 + (7, 8, 9, 10, 11, 12)[k - 16])
                    col_unit(u, u + 1, acc[(2, 3, 0, 1, 2, 3)[k - 16]], xT)
                if k == 17:
                    pe.wait_ge(wf_split, 2)
                    pe.wait_ge(tmpT_done, X_COUNT * (X_PROJ2 + 1))
                    o = aux[1][0:4, 0:ROWS]
                    for kt in range(KT):
                        hi, lo = xT[:, kt, 0:ROWS], xT[:, kt, ROWS:]
                        mm(o, wfh[:, kt, :], hi, start=(kt == 0), stop=False)
                        mm(o, wfh[:, kt, :], lo, start=False, stop=False)
                        ins = mm(o, wfl[:, kt, :], hi, start=False, stop=(kt == KT - 1))
                    ins.then_inc(f_psum, 1)
            for n in range(N_BRANCH):
                for k in range(KT + 2):
                    i = n * (KT + 2) + k
                    u = U_GB + i
                    if k < KT:
                        if k == 0 and n == 0:
                            pe.wait_ge(acc_free, F_PROJ2)
                            wide_half(u, xT[:, k, :], 0, True, False)
                            pe.wait_ge(xc_ready, 2)
                            wide_half(u, xT[:, k, :], 1, True, False).then_inc(unit_done, 1)
                        else:
                            wide_unit(u, xT[:, k, :], k == 0, k == KT - 1, (gated_out, 4 * (n - 1)) if k == 0 else None)
                    else:
                        if k == KT:
                            done, count = ((conv_ready, 2), (y_ready, 2), (sb_ready, 2), (fox_ready, 2))[n]
                            pe.wait_ge(done, count)
                        wide_unit(u, yT[:, 2 * n + k - KT, :], k == KT, k == KT + 1, (sig_done, 4 * n) if k == KT else None)
                    for step, h in steps_at(PE_STEPS, i):
                        if step == "GMIX":
                            pe.wait_ge(vn_ready, 2)
                            pe.wait_ge(ws_ready, 1)
                            for g in range(4):
                                ins = mm(aux[3][:, P * g:P * (g + 1)], wspT[:, g, :], vn[:, :, HD * g:HD * (g + 1)], start=True, stop=True)
                            ins.then_inc(gmix_done, 1)
                        elif step == "GT":
                            pe.wait_ge(yb_ready, 1)
                            for t in range(2):
                                for r in range(RT):
                                    ins = transpose(aux[3][:, ROWS * t + P * r:ROWS * t + P * (r + 1)], yb[:, r, P * t:P * (t + 1)])
                            ins.then_inc(yb_psum, 1)
                        elif step == "CUM":
                            pe.wait_ge(logf_copied, 1)
                            o = aux[1][0:4, 0:ROWS]
                            mm(o, logf[:, 0, :], upper[:, P:3 * P], start=True, stop=False)
                            mm(o, logf[:, 1, :], upper[:, 0:2 * P], start=False, stop=True).then_inc(cum_psum, 1)
                        elif step == "LOGT":
                            pe.wait_ge(logf_ready, 1)
                            for r in range(RT):
                                ins = transpose(aux[1][:, ROWS + 4 * r:ROWS + 4 * r + 4], logfT[:, P * r:P * (r + 1)], 4)
                            ins.then_inc(logf_psum, 1)
                        elif step == "FTQ" or step == "FTK":
                            s = int(step == "FTK")
                            pe.wait_ge(fx_normed, 4)
                            if s == 0:
                                pe.wait_ge(y_ready, 2)
                            for t in range(2):
                                for r in range(RT):
                                    src = (svq[:, r, 256 + P * t:256 + P * (t + 1)], fkv[:, r, P * t:P * (t + 1)])[s]
                                    ins = transpose(aux[3 - s][:, ROWS * t + P * r:ROWS * t + P * (r + 1)], src)
                            ins.then_inc(fx_psum, 1)
                        elif step == "Z":
                            o = HD * (h % 2)
                            q, kk = sbT[o:o + HD, h // 2, :], sbT[o:o + HD, 2 + h // 2, :]
                            if h >= 1:
                                pe.wait_ge(z_copied, h)
                            mm(aux[0][:, 0:ROWS], kk[:, 0:P], q, start=True, stop=True)
                            mm(aux[0][:, ROWS:384], kk[:, P:], q[:, P:], start=True, stop=True).then_inc(z_psum, 1)
                        elif step == "ARG":
                            pe.wait_ge(sp_masked, h + 1)
                            if h == 0:
                                pe.wait_ge(cum_ready, 1)
                            else:
                                pe.wait_ge(arg_made, h)
                            bank, spl = aux[1], probs[:, 0, 0:384]
                            mm(bank[:, 0:ROWS], neg_ge[:, :], spl[:, 0:ROWS], start=True, stop=False)
                            mm(bank[:, P:ROWS], neg_ones[:, :], spl[:, ROWS:384], start=False, stop=True)
                            mm(bank[:, ROWS:384], neg_ge[:, :], spl[:, ROWS:384], start=True, stop=True).then_inc(arg_psum, 1)
                        elif step == "PVS":
                            o = HD * (h % 2)
                            pe.wait_ge(w_masked, h + 1)
                            if h == 0:
                                pe.wait_ge(fxT_ready, 2)
                            if h == 2:
                                pe.wait_ge(sb_ready, 1)
                            mm(aux[2][o:o + HD, 0:ROWS], svq[:, 0, HD * h:HD * (h + 1)], probsT[:, 0, 0:ROWS], start=True, stop=False)
                            mm(aux[2][o:o + HD, P:ROWS], svq[:, 1, HD * h:HD * (h + 1)], probsT[:, 0, ROWS:384],
                               start=False, stop=True).then_inc(pvs_done, 1)
                        elif step == "QK":
                            if h == N_HEADS:
                                pe.wait_ge(z_copied, 4)
                            score(h)
                        elif step == "TR":
                            if h == N_HEADS:
                                pe.wait_ge(arg_made, 4)
                            transpose_probs(h)
                        elif step == "PV":
                            weigh(h)
            pe.wait_ge(fox_ready, 2)
            to_columns(merged, 0, X_OUT2, merged_ready, 4 * (N_BRANCH - 1) - RT)
            for r in range(RT):
                for k in range(RING):
                    if k % 4 == 0:
                        pe.wait_ge(xT_ready, X_COUNT * X_OUT2 + KT * r + 4)
                    ins = wide_half(U_OUT2 + k, xT[:, k, :], r, k == 0, False)
                    if r == 0 and k == 0:
                        to_columns(merged, 1, X_OUT2, merged_ready, 4 * (N_BRANCH - 1))
                    if r == 1:
                        ins.then_inc(unit_done, 1)
            pe.wait_ge(xT_ready, X_COUNT * (X_OUT2 + 1))
            wide_rows(U_OUT2, lambda k: xT[:, k, :], range(RING, KT), 0, None, KT - 1)
            wide_rows(U_OUT2, lambda k: xT[:, k, :], range(RING, KT - 1), 1, None, KT - 1)
            to_columns(xr, 0, X_UP2, normed, 3 * RT + 1)
            wide_rows(U_OUT2, lambda k: xT[:, k, :], range(KT - 1, KT), 1, None, KT - 1)
            to_columns(xr, 1, X_UP2, normed, 3 * RT + 2)
            pe.wait_ge(resid, 3 * RT)
            with pe.Fori(0, FF2 // P // 2) as i:
                for k in range(RING):
                    pe.wait_ge(acc_free, F_PROJ2 - 2 + 2 * (k // 2) + RING * i)
                    col_unit(U_UP2 + k, U_UP2 + k + 1 + RING * i, acc[k], xT, columns_ready(X_UP2) if k == 0 else None)
            n_hid = FF2 // P
            for k in range(n_hid - RING):
                pe.wait_ge(hid_ready, RING + D_FF // P + k + 1)
                wide_unit(U_DOWN2 + k, hid[:, k, :], k == 0, False, (acc_free, F_PROJ2 + 2 * n_hid - 4) if k == 0 else None)
            pe.wait_ge(hid_ready, RING + D_FF // P + n_hid)
            for r in range(RT):
                wide_rows(U_DOWN2, lambda k: hid[:, k, :], range(n_hid - RING, n_hid), r, None, n_hid - 1)


def bucket_table():
    dist = 255 - np.arange(DIST)
    n = np.maximum(dist, 0)
    exact = N_BUCKETS // 2
    large = exact + (np.log(np.maximum(n, 1).astype(np.float32) / exact) / np.float32(np.log(MAX_DISTANCE / exact))
                     * (N_BUCKETS - exact)).astype(np.int32)
    bucket = np.where(n < exact, n, np.minimum(large, N_BUCKETS - 1))
    t = np.zeros((WMASK_ROW + 1, DIST), np.float32)
    t[bucket, np.arange(DIST)] = 1.0
    t[N_BUCKETS, dist < 0] = NEG
    t[WMASK_ROW, dist >= WINDOW] = NEG
    return t


_INS = ["x", "c", "w_in", "w_out", "sinks", "rel_bias", "w_ada", "b_ada", "norm_gains", "w1", "b1", "w2", "b2",
        "norm_mix_g_2", "w_in_2", "w_conv_2", "w_spatial_2", "b_spatial_2", "gmlp_ln_g_2", "gmlp_ln_b_2",
        "fox_q_norm_g_2", "fox_k_norm_g_2", "fox_forget_b_2", "w_branch_2", "w_out_2", "norm_ffn_g_2",
        "w_ffn_in_2", "w_ffn_out_2"]


def kernel(**inputs):
    import concourse.bacc as bacc
    from concourse.bass_utils import run_bass_kernel_spmd

    nc = bacc.Bacc("TRN2", target_bir_lowering=False, num_devices=1)
    arrays, aps = {}, {}
    for name in _INS:
        arr = np.ascontiguousarray(inputs[name])
        arrays["in_" + name] = arr
        aps[name] = nc.dram_tensor("in_" + name, arr.shape, mybir.dt.from_np(arr.dtype), kind="ExternalInput").ap()
    table = bucket_table()
    arrays["bucket_onehot"] = table
    aps["bucket_onehot"] = nc.dram_tensor("bucket_onehot", table.shape, mybir.dt.float32, kind="ExternalInput").ap()
    aps["out"] = nc.dram_tensor("out_rows", (1, ROWS, D), mybir.dt.float32, kind="ExternalOutput").ap()
    build_program(nc, aps)
    r = run_bass_kernel_spmd(nc, [arrays], core_ids=[0])
    return r.results[0]["out_rows"]
```
